# Optimizing a Trainium2 kernel written in Bass

```python
import jax
import jax.numpy as jnp
from jax import lax
import numpy as np

D_MODEL = 1024
BATCH = 1
SEQ = 1024
DEPTH = 1
DEC_BATCH = 8
DEC_SEQ = 4
PAST_LEN = 1024
PAGE_SIZE = 128

HEAD_DIM = 64
MIX_W = D_MODEL
ATT_W = MIX_W // 2
SB_HEADS = ATT_W // HEAD_DIM
SB_BIAS_INIT = -7.0
CONV_CH = MIX_W - ATT_W
CONV_WIDTH = 31
IN_W = 3 * ATT_W + 2 * CONV_CH
Q_BLOCK = 128
N_EXPERTS = 16
N_EXPERT_GROUPS = 4
EXPERTS_PER_GROUP = N_EXPERTS // N_EXPERT_GROUPS
TOP_K = 2
D_EXPERT = D_MODEL // 2
EPS = 1e-6

kernel_name = 'hymba_stickbreak_conformer_moe_step'

def rmsnorm(x, g):
    xf = x.astype(jnp.float32)
    y = xf * lax.rsqrt(jnp.mean(xf * xf, axis=-1, keepdims=True) + EPS)
    return (y * g.astype(jnp.float32)).astype(x.dtype)

def layernorm(x, g, b):
    xf = x.astype(jnp.float32)
    xc = xf - jnp.mean(xf, axis=-1, keepdims=True)
    y = xc * lax.rsqrt(jnp.mean(xc * xc, axis=-1, keepdims=True) + EPS)
    return (y * g.astype(jnp.float32) + b.astype(jnp.float32)).astype(x.dtype)

def adaln(c, w, b):
    m = jnp.einsum('bd,de->be', jax.nn.silu(c), w) + b
    return [t[:, None, :] for t in jnp.split(m, 6, axis=-1)]

def modulate(h, shift, scale):
    return h * (1 + scale) + shift

def mix_project(h, w_in_l, qn, kn):
    bsz, n = h.shape[:2]
    u = jnp.einsum('bnd,de->bne', h, w_in_l)
    q, k, v, ca, cg = jnp.split(u, [ATT_W, 2 * ATT_W, 3 * ATT_W, 3 * ATT_W + CONV_CH], axis=-1)
    heads = lambda t: t.reshape(bsz, n, SB_HEADS, HEAD_DIM)
    q = rmsnorm(heads(q), qn)
    k = rmsnorm(heads(k), kn)
    glu = ca * jax.nn.sigmoid(cg)
    return q, k, heads(v), glu

def stick_breaking(q, k, v, q_pos, k_pos, bias):
    z = jnp.einsum('bqhd,bkhd->bhqk', q, k, preferred_element_type=jnp.float32) * (HEAD_DIM ** -0.5)
    z = z + bias.astype(jnp.float32)[None, :, None, None]
    mask = k_pos[None, :] < q_pos[:, None]
    log_keep = jnp.where(mask, jax.nn.log_sigmoid(-z), 0.0)
    log_between = lax.cumsum(log_keep, axis=3, reverse=True) - log_keep
    a = jnp.where(mask, jnp.exp(jax.nn.log_sigmoid(z) + log_between), 0.0)
    return jnp.einsum('bhqk,bkhd->bqhd', a.astype(v.dtype), v)

def sb_prompt(q, k, v, bias):
    bsz, n = q.shape[:2]
    nb = n // Q_BLOCK
    pos = jnp.arange(n)
    qb = q.reshape(bsz, nb, Q_BLOCK, SB_HEADS, HEAD_DIM).swapaxes(0, 1)
    pb = pos.reshape(nb, Q_BLOCK)
    ob = lax.map(lambda a: stick_breaking(a[0], k, v, a[1], pos, bias), (qb, pb))
    return ob.swapaxes(0, 1).reshape(bsz, n, SB_HEADS, HEAD_DIM)

def conv_module(glu_ext, w, b, ln_g, ln_b):
    y = lax.conv_general_dilated(glu_ext, w[:, None, :].astype(glu_ext.dtype), (1,), 'VALID',
                                 dimension_numbers=('NWC', 'WIO', 'NWC'),
                                 feature_group_count=CONV_CH) + b
    return jax.nn.silu(layernorm(y, ln_g, ln_b))

def mix_merge(att, cv, w_out_l):
    bsz, n = att.shape[:2]
    cat = jnp.concatenate([att.reshape(bsz, n, ATT_W), cv], axis=-1)
    return jnp.einsum('bne,ed->bnd', cat, w_out_l)

def moe(h, w_router, b_router, wg, wu, wd):
    shape = h.shape
    t = h.reshape(-1, D_MODEL)
    n = t.shape[0]
    logits = jnp.einsum('nd,de->ne', t, w_router, preferred_element_type=jnp.float32)
    probs = jax.nn.softmax(logits, axis=-1)
    sel = probs + b_router.astype(jnp.float32)
    grp_score = lax.top_k(sel.reshape(n, N_EXPERT_GROUPS, EXPERTS_PER_GROUP), TOP_K)[0].sum(-1)
    best = jnp.argmax(grp_score, axis=-1)
    in_grp = (jnp.arange(N_EXPERTS) // EXPERTS_PER_GROUP)[None, :] == best[:, None]
    _, idx = lax.top_k(jnp.where(in_grp, sel, -jnp.inf), TOP_K)
    p_sel = jnp.take_along_axis(probs, idx, axis=-1)
    w = p_sel / jnp.sum(p_sel, axis=-1, keepdims=True)
    gates = jnp.sum(jax.nn.one_hot(idx, N_EXPERTS, dtype=jnp.float32) * w[..., None], axis=1)
    a = jnp.einsum('nd,edf->nef', t, wg)
    b = jnp.einsum('nd,edf->nef', t, wu)
    act = jax.nn.silu(a) * b * gates[:, :, None].astype(t.dtype)
    return jnp.einsum('nef,efd->nd', act, wd).reshape(shape)

def ffn_sublayer(x, shift, scale, gate, g, w_router, b_router, wg, wu, wd):
    h = modulate(rmsnorm(x, g), shift, scale)
    return x + gate * moe(h, w_router, b_router, wg, wu, wd)

def setup_inputs(seed: int = 0) -> dict:
    key = jax.random.key(seed)
    ks = jax.random.split(key, 32)
    f32 = jnp.float32
    n_pages = PAST_LEN // PAGE_SIZE
    n_used = DEC_BATCH * n_pages
    n_pool = n_used + n_used // 4
    nrm = lambda k, shape, s: jax.random.normal(k, shape, f32) * s
    page_table = jax.random.permutation(ks[5], n_pool)[:n_used].reshape(DEC_BATCH, n_pages).astype(jnp.int32)
    return {
        'x_prompt': nrm(ks[0], (BATCH, SEQ, D_MODEL), 1.0),
        'x_sample': nrm(ks[1], (DEC_BATCH, DEC_SEQ, D_MODEL), 1.0),
        'cache_k': nrm(ks[2], (DEPTH, n_pool, PAGE_SIZE, SB_HEADS, HEAD_DIM), 1.0),
        'cache_v': nrm(ks[3], (DEPTH, n_pool, PAGE_SIZE, SB_HEADS, HEAD_DIM), 1.0),
        'state_conv': nrm(ks[4], (DEPTH, DEC_BATCH, CONV_WIDTH - 1, CONV_CH), 0.5),
        'page_table': page_table,
        'c_prompt': nrm(ks[6], (BATCH, D_MODEL), 1.0),
        'c_sample': nrm(ks[7], (DEC_BATCH, D_MODEL), 1.0),
        'w_ada': nrm(ks[8], (DEPTH, D_MODEL, 6 * D_MODEL), 0.5 * D_MODEL ** -0.5),
        'b_ada': nrm(ks[9], (DEPTH, 6 * D_MODEL), 0.02),
        'norm_mix': 1.0 + nrm(ks[10], (DEPTH, D_MODEL), 0.05),
        'norm_ffn': 1.0 + nrm(ks[11], (DEPTH, D_MODEL), 0.05),
        'w_in': nrm(ks[12], (DEPTH, D_MODEL, IN_W), D_MODEL ** -0.5),
        'q_norm': 1.0 + nrm(ks[13], (DEPTH, HEAD_DIM), 0.05),
        'k_norm': 1.0 + nrm(ks[14], (DEPTH, HEAD_DIM), 0.05),
        'sb_bias': SB_BIAS_INIT + nrm(ks[25], (DEPTH, SB_HEADS), 0.1),
        'conv_w': nrm(ks[15], (DEPTH, CONV_WIDTH, CONV_CH), CONV_WIDTH ** -0.5),
        'conv_b': nrm(ks[16], (DEPTH, CONV_CH), 0.02),
        'conv_ln_g': 1.0 + nrm(ks[17], (DEPTH, CONV_CH), 0.05),
        'conv_ln_b': nrm(ks[18], (DEPTH, CONV_CH), 0.02),
        'w_out': nrm(ks[19], (DEPTH, MIX_W, D_MODEL), MIX_W ** -0.5),
        'w_router': nrm(ks[20], (D_MODEL, N_EXPERTS), D_MODEL ** -0.5),
        'b_router': nrm(ks[21], (N_EXPERTS,), 0.01),
        'w_gate': nrm(ks[22], (DEPTH, N_EXPERTS, D_MODEL, D_EXPERT), D_MODEL ** -0.5),
        'w_up': nrm(ks[23], (DEPTH, N_EXPERTS, D_MODEL, D_EXPERT), D_MODEL ** -0.5),
        'w_down': nrm(ks[24], (DEPTH, N_EXPERTS, D_EXPERT, D_MODEL), D_EXPERT ** -0.5),
    }

def reference(x_prompt, x_sample, cache_k, cache_v, state_conv, page_table, c_prompt, c_sample,
              w_ada, b_ada, norm_mix, norm_ffn, w_in, q_norm, k_norm, sb_bias, conv_w, conv_b, conv_ln_g,
              conv_ln_b, w_out, w_router, b_router, w_gate, w_up, w_down):
    dec_b, n_dec = x_sample.shape[:2]
    past_len = page_table.shape[1] * cache_k.shape[2]
    q_pos_s = past_len + jnp.arange(n_dec)
    k_pos_s = jnp.arange(past_len + n_dec)
    xp, xs = x_prompt, x_sample
    kp_l, vp_l, cp_l, ks_l, vs_l, cs_l = [], [], [], [], [], []
    for l in range(DEPTH):
        sh1p, sc1p, g1p, sh2p, sc2p, g2p = adaln(c_prompt, w_ada[l], b_ada[l])
        sh1s, sc1s, g1s, sh2s, sc2s, g2s = adaln(c_sample, w_ada[l], b_ada[l])

        hp = modulate(rmsnorm(xp, norm_mix[l]), sh1p, sc1p)
        q, k, v, glu = mix_project(hp, w_in[l], q_norm[l], k_norm[l])
        att = sb_prompt(q, k, v, sb_bias[l])
        glu_ext = jnp.pad(glu, ((0, 0), (CONV_WIDTH - 1, 0), (0, 0)))
        cv = conv_module(glu_ext, conv_w[l], conv_b[l], conv_ln_g[l], conv_ln_b[l])
        xp = xp + g1p * mix_merge(att, cv, w_out[l])
        kp_l.append(k)
        vp_l.append(v)
        cp_l.append(glu_ext[:, -(CONV_WIDTH - 1):])

        hs = modulate(rmsnorm(xs, norm_mix[l]), sh1s, sc1s)
        q, k, v, glu = mix_project(hs, w_in[l], q_norm[l], k_norm[l])
        k_past = cache_k[l][page_table].reshape(dec_b, past_len, SB_HEADS, HEAD_DIM)
        v_past = cache_v[l][page_table].reshape(dec_b, past_len, SB_HEADS, HEAD_DIM)
        att = stick_breaking(q, jnp.concatenate([k_past, k], axis=1),
                             jnp.concatenate([v_past, v], axis=1), q_pos_s, k_pos_s, sb_bias[l])
        glu_ext = jnp.concatenate([state_conv[l], glu], axis=1)
        cv = conv_module(glu_ext, conv_w[l], conv_b[l], conv_ln_g[l], conv_ln_b[l])
        xs = xs + g1s * mix_merge(att, cv, w_out[l])
        ks_l.append(k)
        vs_l.append(v)
        cs_l.append(glu_ext[:, -(CONV_WIDTH - 1):])

        xp = ffn_sublayer(xp, sh2p, sc2p, g2p, norm_ffn[l], w_router, b_router, w_gate[l], w_up[l], w_down[l])
        xs = ffn_sublayer(xs, sh2s, sc2s, g2s, norm_ffn[l], w_router, b_router, w_gate[l], w_up[l], w_down[l])

    return (xp, xs, jnp.stack(kp_l), jnp.stack(vp_l), jnp.stack(cp_l),
            jnp.stack(ks_l), jnp.stack(vs_l), jnp.stack(cs_l))


_drawn_inputs = setup_inputs


def setup_inputs(seed=0):
    import zlib

    import numpy as np

    out = dict(_drawn_inputs(seed))
    spreads = {}
    factors = {'cache_k': 7.533,
     'cache_v': 5.912,
     'q_norm': 8.0,
     'sb_bias': 6.979,
     'conv_b': 5.156,
     'conv_ln_g': 4.128,
     'conv_ln_b': 8.0}
    for name, (base, spread) in spreads.items():
        noise = np.random.default_rng([zlib.crc32(name.encode()), seed]).standard_normal(out[name].shape)
        drawn = base * np.exp(spread * noise) if base else spread * noise
        out[name] = jnp.asarray(drawn.astype(out[name].dtype))
    for name, factor in factors.items():
        out[name] = (out[name] * factor).astype(out[name].dtype)
    return out
```

```python
from contextlib import ExitStack

import concourse.bass as bass
from concourse import mybir

F32 = mybir.dt.float32
BF16 = mybir.dt.bfloat16
I32 = mybir.dt.int32
ALU = mybir.AluOpType
ACT = mybir.ActivationFunctionType
AX_X = mybir.AxisListType.X

P = 128
EPS = 1e-6
NEG = -1.0e30


class Chain:

    def __init__(self, eng, sem):
        self.eng, self.sem, self.n = eng, sem, 0

    def put(self, ins):
        self.n += 1
        ins.then_inc(self.sem, 1)

    def wait(self, back=0):
        if self.n - back > 0:
            self.eng.wait_ge(self.sem, self.n - back)

    def reset(self):
        self.wait()
        self.eng.sem_clear(self.sem)
        self.n = 0


def decoder_step(nc, x_prompt, x_sample, cache_k, cache_v, state_conv, page_table, c_prompt, c_sample,
                 w_ada, b_ada, norm_mix, norm_ffn, w_in, q_norm, k_norm, sb_bias, conv_w, conv_b, conv_ln_g,
                 conv_ln_b, w_out, w_router, b_router, w_gate, w_up, w_down,
                 y_prompt, y_sample, new_k_prompt, new_v_prompt, new_conv_prompt,
                 new_k_sample, new_v_sample, new_conv_sample):
    SEQ, D = x_prompt.shape[1:]
    DB, DS = x_sample.shape[:2]
    NS = DB * DS
    NPOOL, PAGE, H, HD = cache_k.shape[1:]
    NPG = page_table.shape[1]
    PAST = NPG * PAGE
    AW = H * HD
    CW, CC = conv_w.shape[1:]
    TAIL = CW - 1
    E, _, F = w_gate.shape[1:]
    EG = 4
    EPG = E // EG
    KD = D // P
    NTP = SEQ // P
    NT = NTP + 1
    TOK = SEQ + NS
    NPAIR = H // 2
    NCH = CC // P
    NCHUNK = w_in.shape[2] // 512
    NADA = w_ada.shape[2] // D
    MT = (2 * TOK + E * (P - 1)) // P
    MT += MT % 2
    NSLOT = MT * P
    MT_USED = (2 * TOK + 2 * P - 1) // (2 * P) * 2
    KF = F // P
    assert AW == 512 and CC == 512 and D == 1024 and PAGE == P and NS == 32 and F == 512

    mods_d = nc.dram_tensor("mods_d", [1 + DB, NADA * D], F32).ap()
    qT_d = nc.dram_tensor("qT_d", [NPAIR, P, SEQ], F32).ap()
    kT_d = nc.dram_tensor("kT_d", [NPAIR, P, SEQ], F32).ap()
    h2_d = nc.dram_tensor("h2_d", [TOK, D], F32).ap()
    slot_tok_d = nc.dram_tensor("slot_tok_d", [NSLOT, 1], I32).ap()
    y_d = nc.dram_tensor("y_d", [NSLOT, D], F32).ap()

    xp, xs = x_prompt[0], x_sample.rearrange("a b d -> (a b) d")
    yp, ys = y_prompt[0], y_sample.rearrange("a b d -> (a b) d")
    kp_out = new_k_prompt[0, 0].rearrange("n h d -> n (h d)")
    vp_out = new_v_prompt[0, 0].rearrange("n h d -> n (h d)")
    ks_out = new_k_sample[0].rearrange("b n h d -> (b n) (h d)")
    vs_out = new_v_sample[0].rearrange("b n h d -> (b n) (h d)")
    ck = cache_k[0].rearrange("n p h d -> n p (h d)")
    cv = cache_v[0].rearrange("n p h d -> n p (h d)")

    def rows_of(vec, parts, reps=1, width=None, offset=0):
        width = width or vec.shape[-1]
        return bass.AP(vec.tensor, vec.offset + offset, [[0, parts], [0, reps], [1, width]])

    ctx = ExitStack()
    with ctx:
        def sb(name, shape, dt=F32):
            return ctx.enter_context(nc.sbuf_tensor(name, shape, dt))

        def sem(name):
            return ctx.enter_context(nc.semaphore(name))

        big = sb("big", [P, 24576])
        mid = sb("mid", [P, 8192])
        low = sb("low", [P, 9400])
        cvT = sb("cvT", [P, NCH, TOK])
        xt = sb("xt", [P, 2, D])
        G2 = sb("G2", [P, 2, D])
        identf = sb("identf", [P, P])
        identb = sb("identb", [P, P], BF16)
        causal = sb("causal", [P, P], BF16)
        before = sb("before", [P, P], BF16)
        onesb = sb("onesb", [P, P], BF16)
        q_of_row = sb("q_of_row", [DS, H, DS], BF16)
        mean_of = sb("mean_of", [P, P])
        mhalf = sb("mhalf", [P, 16])
        cT = sb("cT", [P, KD, 16])
        cw = sb("cw", [P, NCH, 36])
        bb = sb("bb", [P, H])
        nbb = sb("nbb", [P, H])
        bs = sb("bs", [NS, 1])
        nbs = sb("nbs", [NS, 1])
        pt = sb("pt", [1, DB * NPG], I32)
        st = sb("st", [P, 64])
        qTs = sb("qTs", [P, NPAIR, NS])
        kTs = sb("kTs", [P, NPAIR, NS])
        wr = sb("wr", [P, KD, E])
        br = sb("br", [P, E])
        logits = sb("logits", [P, NT, E])
        tok_id = sb("tok_id", [P, NT], I32)
        slot_i = sb("slot_i", [P, 2, NT], I32)
        wgt = sb("wgt", [P, 2, NT])
        tile_exp = sb("tile_exp", [P, MT], I32)
        n_pairs = sb("n_pairs", [P, 1], I32)
        NCAP = (TOK + P - 1) // P
        ramp_i = sb("ramp_i", [P, MT + EG + E + NCAP], I32)
        ramp = sb("ramp", [P, MT + EG + E + NCAP])
        tile_no, g_rank = ramp[:, 0:MT], ramp[:, MT:MT + EG]
        e_rank, cap_no = ramp[:, MT + EG:MT + EG + E], ramp[:, MT + EG + E:]
        col_tok = sb("col_tok", [P, 2], I32)
        zcol = sb("zcol", [P, MT], I32)
        bank = ctx.enter_context(nc.psum_tensor("bank", [P, 8, 512], F32))
        flat = bank[:, :, :].rearrange("p b n -> p (b n)")

        ada = mid[:, :].rearrange("p (s k n) -> p s k n", s=4, k=4)
        A0 = 20480
        w_in_sb = big[:, 0:A0].rearrange("p (k n) -> p k n", k=KD)
        c9 = big[0:1 + DB, A0:A0 + D]
        csig = big[0:1 + DB, A0 + D:A0 + 2 * D]
        mrow = big[0:1 + DB, A0 + 2 * D:A0 + 3 * D]
        brow = big[0:1 + DB, A0 + 3 * D:A0 + 4 * D]
        hrow = big[:, A0:A0 + 2 * D].rearrange("p (s n) -> p s n", s=2)
        hT = big[:, A0 + 2 * D:A0 + 4 * D].rearrange("p (s k n) -> p s k n", s=2, k=KD)
        qk_t = mid[:, 0:2048].rearrange("p (s n) -> p s n", s=2)
        v_t = mid[:, 2048:3072].rearrange("p (s n) -> p s n", s=2)
        glu_t = mid[:, 3072:4096].rearrange("p (s n) -> p s n", s=2)
        sg_t = mid[:, 4096:5120].rearrange("p (s n) -> p s n", s=2)
        sq_t = mid[:, 5120:6144]
        qT_t = mid[:, 6144:6656]
        kT_t = mid[:, 6656:7168]
        qkw = mid[:, 7168:8192]
        GX = TAIL + SEQ
        glu_x = low[:, 0:NCH * GX].rearrange("p (c n) -> p c n", c=NCH)
        SX = TAIL + DS
        G0 = NCH * GX
        glu_s = low[:, G0:G0 + NCH * DB * SX].rearrange("p (c b n) -> p c b n", c=NCH, b=DB)
        B0 = G0 + NCH * DB * SX
        AB = low[:, B0:B0 + 4 * D].rearrange("p (s w n) -> p s w n", s=2, w=2)
        ln_a = big[:, 0:2048].rearrange("p (c n) -> p c n", c=NCH)
        ln_b = big[:, 2048:4096].rearrange("p (c n) -> p c n", c=NCH)
        ln_v = big[:, 4096:4608]
        ln_r = big[:, 4608:5120]
        stage = big[:, 0:6144].rearrange("p (s w n) -> p s w n", s=2, w=3)
        sig = big[:, 6144:8192].rearrange("p (s n) -> p s n", s=2)
        keep = big[:, 8192:10240].rearrange("p (s n) -> p s n", s=2)
        prod = big[:, 10240:12292].rearrange("p (s n) -> p s n", s=2)
        aT = big[:, 12292:14340].rearrange("p (s n) -> p s n", s=2)
        O0 = 24576 - NPAIR * TOK
        oT = big[:, O0:].rearrange("p (c n) -> p c n", c=NPAIR)
        KN = PAST + DS
        k_pg = big[:, 0:8192].rearrange("p (s g n) -> p s g n", s=2, g=NPG)
        v_pg = big[:, 8192:16384].rearrange("p (s g n) -> p s g n", s=2, g=NPG)
        sig_s = big[0:NS, 16384:16384 + KN]
        keep_s = big[0:NS, 17412:17412 + KN]
        prod_s = big[0:NS, 18440:18440 + KN + 1]
        aT_s = big[:, 19470:19470 + 9 * NS].rearrange("p (g n) -> p g n", n=NS)
        v_new = xt[0:DS, 1, :].rearrange("p (s n) -> p s n", s=2)
        q_bd = xt[:, 0, :].rearrange("p (b c n) -> p b c n", b=DB, c=NPAIR)
        q_stage = sb("q_stage", [P, NPAIR, NS])
        kT = low[:, 0:NPAIR * KN].rearrange("p (c n) -> p c n", c=NPAIR)
        w_out_sb = mid[:, :].rearrange("p (k n) -> p k n", k=KD)
        mod2 = big[:, 0:6144].rearrange("p (w s n) -> p w s n", w=3, s=2)
        h2 = big[:, 6144:8192].rearrange("p (s n) -> p s n", s=2)
        h2T = big[:, 8192:10240].rearrange("p (s k n) -> p s k n", s=2, k=KD)
        sqx = big[:, 10240:11264]
        gffn = big[:, 11264:12288]
        x1 = low[:, 0:NT * D].rearrange("p (t n) -> p t n", t=NT)
        R0 = [4096]

        def small(*shape):
            n = 1
            for k in shape:
                n *= k
            v = mid[:, R0[0]:R0[0] + n]
            R0[0] += n
            if len(shape) == 2:
                v = v.rearrange("p (a b) -> p a b", a=shape[0])
            if len(shape) == 3:
                v = v.rearrange("p (a b c) -> p a b c", a=shape[0], b=shape[1])
            return v

        r_a, r_b = small(NT), small(NT)
        r_z, r_e, r_p, r_sel, r_off, r_h0, r_h1, r_valid = (small(NT, E) for _ in range(8))
        r_hi, r_lo = small(NT * EG * 2), small(NT * EG * 2)
        r_gs, r_g1 = small(NT * EG), small(NT * EG)
        r_cmp = small(MT * E)
        r_base = small(NT + 1, E)
        r_nt, r_end, r_t1 = small(E), small(E), small(E)
        r_te = small(MT)
        assert R0[0] <= 8192
        r_maskb = sb("r_maskb", [P, NT * E], BF16)[:, :]
        r_mask3 = r_maskb.rearrange("p (t e) -> p t e", e=E)
        wts = big[:, :].rearrange("p (s n) -> p s n", s=2)
        wg_sb = wts[:, :, 0:4096].rearrange("p s (k n) -> p s k n", k=KD)
        wu_sb = wts[:, :, 4096:8192].rearrange("p s (k n) -> p s k n", k=KD)
        wd_sb = wts[:, :, 8192:12288].rearrange("p s (k n) -> p s k n", k=KF)
        xg = mid[:, 0:2048].rearrange("p (s n) -> p s n", s=2)
        xgT = mid[:, 2048:4096].rearrange("p (s k n) -> p s k n", s=2, k=KD)
        act_t = mid[:, 4096:5120].rearrange("p (s n) -> p s n", s=2)
        actT = mid[:, 5120:6144].rearrange("p (s k n) -> p s k n", s=2, k=KF)
        y_t = mid[:, 6144:8192].rearrange("p (s n) -> p s n", s=2)
        ya = big[:, 0:NT * D].rearrange("p (t n) -> p t n", t=NT)
        yb = big[:, NT * D:2 * NT * D].rearrange("p (t n) -> p t n", t=NT)

        phase = sem("phase")
        settled = sem("settled")
        names = ("const_in pool_const c_sig c_silu cT_ps cT_sb st_ps st_sb w_in_in brow_in ada_used ada_mm rows_done "
                 "rows_stored mod1_in mod1_done "
                 "x_sq x_var x_rstd h_ready hT_ps hT_sb mm_chunk sg_done glu_done qk_sq qk_var qk_rstd qk_scaled "
                 "qk_done v_done post_ps glu_sb q_sb k_sb qkT_st conv_st conv_done "
                 "ln_mean ln_cent ln_sq ln_var ln_dv ln_std ln_norm ln_sig ln_done "
                 "qk_mm keep_done sig_done scan_done a_done at_ps at_sb pv_mm o_sb w_out_in zero_idx zero_y "
                 "kt_ps kt_act kt_dve q_staged qbd_done s_mm s_keep s_sig s_scan s_a s_at s_at_sb s_pv s_o "
                 "mod2_in mod2_done mix_mm x1_tmp x1_done x2_sq x2_var x2_rstd h2_done h2_ps h2T_sb lg_mm lg_sb "
                 "h2_st r_pos r_m r_slots tok_st exp_ready tiles_ready "
                 "xg_ps xgT_sb xgT_hi gu_mm g_sig act_done aT_ps aT_sb y_mm y_lo y_hi y_first y_sum out_st "
                 "dve_c act_c pool_c").split()
        S = {n: sem(n) for n in names}
        ada_in = [sem(f"ada_in{i}") for i in range(4)]
        x_in = [sem(f"x_in{i}") for i in range(2)]
        kv_st = [sem(f"kv_st{i}") for i in range(2)]
        stage_in = [sem(f"stage_in{i}") for i in range(2)]
        k_in = [sem(f"k_in{i}") for i in range(2)]
        v_in = [sem(f"v_in{i}") for i in range(2)]
        x2_in = [sem(f"x2_in{i}") for i in range(2)]
        h2_stored = [sem(f"h2_stored{i}") for i in range(2)]
        wg_in = [sem(f"wg_in{i}") for i in range(2)]
        wu_in = [sem(f"wu_in{i}") for i in range(2)]
        wd_in = [sem(f"wd_in{i}") for i in range(2)]
        col_in = [sem(f"col_in{i}") for i in range(2)]
        xg_in = [sem(f"xg_in{i}") for i in range(2)]
        y_st = [sem(f"y_st{i}") for i in range(2)]
        ya_in = [sem(f"ya_in{i}") for i in range(NT)]

        ENGINES = 5
        N_CONST = 13
        LN_COLS = [(c0, min(512, TOK - c0)) for c0 in range(0, TOK, 512)]

        def join(eng, n):
            eng.drain().then_inc(phase, 1)
            eng.wait_ge(phase, ENGINES * n)

        def settle(eng):
            eng.sem_inc(settled, 1)

        block = ctx.enter_context(nc.Block())
        UNITS = 2 * NTP

        @block.sync
        def _(sp):
            n_const = [0]

            def const(dst, src):
                n_const[0] += 16
                sp.dma_start(dst, src).then_inc(S["const_in"], 16)

            const(c9[0:1, :], c_prompt)
            const(c9[1:1 + DB, :], c_sample)
            const(xt[0:CW, 0, 0:CC], conv_w[0])
            const(xt[CW:CW + 1, 0, 0:CC], conv_b)
            const(xt[CW + 1:CW + 2, 0, 0:CC], conv_ln_g)
            const(xt[CW + 2:CW + 3, 0, 0:CC], conv_ln_b)
            half_b = DB // 2
            for j in range(2):
                const(xt[0:half_b * TAIL, 1, j * CC:(j + 1) * CC],
                      state_conv[0, j * half_b:(j + 1) * half_b].rearrange("b n c -> (b n) c"))
            const(bb[:, :], bass.AP(sb_bias.tensor, 0, [[0, P], [1, H]]))
            const(bs[:, :], bass.AP(sb_bias.tensor, 0, [[1, H], [0, DS], [1, 1]]))
            const(pt[:, :], page_table.rearrange("b g -> (b g)").rearrange("(a n) -> a n", a=1))
            const(wr[:, :, :], w_router.rearrange("(k p) e -> p k e", p=P))
            const(br[:, :], bass.AP(b_router.tensor, 0, [[0, P], [1, E]]))
            assert n_const[0] == 16 * N_CONST
            with sp.Fori(0, NADA) as i:
                for s in range(4):
                    c, kh = s // 2, s % 2
                    sp.wait_ge(S["ada_used"], 4 * i + s + 1)
                    sp.dma_start(ada[:, s, :, :],
                                 w_ada[0, kh * 512:(kh + 1) * 512, bass.ds(i * D + c * 512, 512)]
                                 .rearrange("(k p) n -> p k n", p=P)).then_inc(ada_in[s], 16)
                sp.wait_ge(S["rows_done"], 2 * i + 2)
                sp.dma_start(brow, bass.AP(b_ada.tensor, 0, [[0, 1 + DB], [1, NADA * D]])[:, bass.ds(i * D, D)])\
                    .then_inc(S["brow_in"], 16)
            for k in range(KD):
                sp.dma_start(w_in_sb[:, k, :], w_in[0, k * P:(k + 1) * P, :]).then_inc(S["w_in_in"], 16)
            sp.wait_ge(S["rows_stored"], 16 * (NADA + 1))
            def mod_rows(dst, w, kind):
                if kind == 0:
                    src = bass.AP(mods_d.tensor, w * D, [[0, P], [1, D]])
                else:
                    src = bass.AP(mods_d.tensor, NADA * D + w * D, [[NADA * D, DB], [0, DS], [1, D]])
                return dst, src
            for kind, parts in ((0, P), (1, NS)):
                for w in range(2):
                    sp.dma_start(*mod_rows(AB[0:parts, kind, w, :], 1 - w, kind)).then_inc(S["mod1_in"], 16)
            sp.dma_start(hrow[:, 0, :], bass.AP(norm_mix.tensor, 0, [[0, P], [1, D]])).then_inc(S["mod1_in"], 16)
            sp.dma_start(qkw[:, 0:AW].rearrange("p (h d) -> p h d", h=H), rows_of(q_norm, P, H)).then_inc(S["mod1_in"], 16)
            sp.dma_start(qkw[:, AW:].rearrange("p (h d) -> p h d", h=H), rows_of(k_norm, P, H)).then_inc(S["mod1_in"], 16)
            join(sp, 1)

            def load_x(t):
                s = t % 2
                if t >= 2:
                    sp.wait_ge(S["h_ready"], t - 1)
                if t < NTP:
                    sp.dma_start(xt[:, s, :], xp[t * P:(t + 1) * P, :]).then_inc(x_in[s], 16)
                elif t == NTP:
                    sp.dma_start(xt[0:NS, s, :], xs).then_inc(x_in[s], 16)

            def store_tile(t):
                s = t % 2
                n = P if t < NTP else NS
                ko, vo = (kp_out[t * P:(t + 1) * P, :], vp_out[t * P:(t + 1) * P, :]) if t < NTP else (ks_out, vs_out)
                sp.wait_ge(S["qk_done"], t + 1)
                sp.dma_start(ko, qk_t[0:n, s, AW:]).then_inc(kv_st[s], 16)
                sp.wait_ge(S["v_done"], t + 1)
                sp.dma_start(vo, v_t[0:n, s, :]).then_inc(kv_st[s], 16)
                if t == NTP - 1:
                    sp.dma_start(new_conv_prompt[0, 0], glu_t[P - TAIL:P, s, :]).then_inc(S["conv_st"], 16)
                if t == NTP:
                    for b in range(DB):
                        sp.dma_start(new_conv_sample[0, b, TAIL - DS:TAIL, :], glu_t[DS * b:DS * b + DS, s, :])\
                            .then_inc(S["conv_st"], 16)
                        sp.dma_start(new_conv_sample[0, b, 0:TAIL - DS, :], state_conv[0, b, DS:TAIL, :])\
                            .then_inc(S["conv_st"], 16)
                if t < NTP:
                    sp.wait_ge(S["q_sb"], t + 1)
                    sp.dma_start(qT_d.rearrange("c p n -> p c n")[:, :, t * P:(t + 1) * P],
                                 qT_t.rearrange("p (c n) -> p c n", c=NPAIR)).then_inc(S["qkT_st"], 16)
                    sp.wait_ge(S["k_sb"], t + 1)
                    sp.dma_start(kT_d.rearrange("c p n -> p c n")[:, :, t * P:(t + 1) * P],
                                 kT_t.rearrange("p (c n) -> p c n", c=NPAIR)).then_inc(S["qkT_st"], 16)

            load_x(0)
            load_x(1)
            for t in range(NT):
                load_x(t + 2)
                if t >= 1:
                    store_tile(t - 1)
            store_tile(NT - 1)
            sp.wait_ge(kv_st[0], 32 * 5)
            sp.wait_ge(kv_st[1], 32 * 4)
            sp.wait_ge(S["qkT_st"], 32 * NTP)
            sp.wait_ge(S["conv_st"], 16 * (1 + 2 * DB))
            join(sp, 2)
            join(sp, 3)

            for k in range(KD):
                sp.dma_start(w_out_sb[:, k, :], w_out[0, k * P:(k + 1) * P, :]).then_inc(S["w_out_in"], 16)
            with sp.Fori(0, NPAIR // 2) as i:
                for s in range(2):
                    pair = 2 * i + s
                    sp.wait_ge(S["pv_mm"], i * 2 * UNITS + s * UNITS + 2)
                    sp.dma_start(stage[:, s, 0, :], qT_d[bass.ds(pair, 1), :, :].rearrange("a p n -> (a p) n"))\
                        .then_inc(stage_in[s], 16)
                    sp.dma_start(stage[:, s, 1, :], kT_d[bass.ds(pair, 1), :, :].rearrange("a p n -> (a p) n"))\
                        .then_inc(stage_in[s], 16)
                    sp.dma_start(stage[:, s, 2, :].rearrange("p (b n) -> p b n", b=NTP),
                                 vp_out[:, bass.ds(pair * P, P)].rearrange("(b p) n -> p b n", p=P))\
                        .then_inc(stage_in[s], 16)
            join(sp, 4)

            with sp.Fori(0, DB // 2) as i:
                for s in range(2):
                    b = 2 * i + s
                    pages = [sp.value_load(pt[0:1, bass.ds(b * NPG + g, 1)], min_val=0, max_val=NPOOL - 1)
                             for g in range(NPG)]
                    sp.wait_ge(S["kt_ps"], NPG * b + NPG)
                    for g in range(NPG):
                        sp.dma_start(k_pg[:, s, g, :], ck[bass.ds(pages[g], 1), :, :].rearrange("a p n -> (a p) n"))\
                            .then_inc(k_in[s], 16)
                    sp.wait_ge(S["s_pv"], b + 1)
                    for g in range(NPG):
                        sp.dma_start(v_pg[:, s, g, :], cv[bass.ds(pages[g], 1), :, :].rearrange("a p n -> (a p) n"))\
                            .then_inc(v_in[s], 16)
                    sp.dma_start(v_new[:, s, :], vs_out[bass.ds(b * DS, DS), :]).then_inc(v_in[s], 16)
            join(sp, 5)

            for w in range(3):
                for kind, parts in ((0, P), (1, NS)):
                    sp.dma_start(*mod_rows(mod2[0:parts, w, kind, :], (2, 4, 3)[w], kind)).then_inc(S["mod2_in"], 16)
            for kind, parts in ((0, P), (1, NS)):
                sp.dma_start(*mod_rows(G2[0:parts, kind, :], 5, kind)).then_inc(S["mod2_in"], 16)
            sp.dma_start(gffn, bass.AP(norm_ffn.tensor, 0, [[0, P], [1, D]])).then_inc(S["mod2_in"], 16)

            def load_x2(t):
                s = t % 2
                if t >= 2:
                    sp.wait_ge(S["x1_done"], t - 1)
                n, src = (P, xp[t * P:(t + 1) * P, :]) if t < NTP else (NS, xs)
                sp.dma_start(xt[0:n, s, :], src).then_inc(x2_in[s], 16)

            def store_h2(t):
                n = P if t < NTP else NS
                sp.wait_ge(S["h2_done"], t + 1)
                sp.dma_start(h2_d[t * P:t * P + n, :], h2[0:n, t % 2, :]).then_inc(h2_stored[t % 2], 16)

            load_x2(0)
            load_x2(1)
            for t in range(NT):
                if t + 2 < NT:
                    load_x2(t + 2)
                store_h2(t)
            sp.wait_ge(h2_stored[0], 16 * 5)
            sp.wait_ge(h2_stored[1], 16 * 4)
            join(sp, 6)
            sp.wait_ge(S["tiles_ready"], 1)
            pairs_used = sp.value_load(n_pairs[0:1, 0:1], min_val=1, max_val=MT // 2)

            with sp.Fori(0, MT // 2) as i, sp.If(i < pairs_used):
                experts = [sp.value_load(tile_exp[0:1, bass.ds(2 * i + s, 1)], min_val=0, max_val=E - 1)
                           for s in range(2)]
                for s in range(2):
                    e = bass.ds(experts[s], 1)
                    sp.wait_ge(S["gu_mm"], 2 * i + s + 1)
                    sp.dma_start(wg_sb[:, s, :, :], w_gate[0, e, :, :].rearrange("a (k p) n -> p (a k) n", p=P))\
                        .then_inc(wg_in[s], 16)
                    sp.dma_start(wu_sb[:, s, :, :], w_up[0, e, :, :].rearrange("a (k p) n -> p (a k) n", p=P))\
                        .then_inc(wu_in[s], 16)
                for s in range(2):
                    e = bass.ds(experts[s], 1)
                    sp.wait_ge(S["y_mm"], 4 * i + 2 * s + 2)
                    sp.dma_start(wd_sb[:, s, :, :], w_down[0, e, :, :].rearrange("a (k p) n -> p (a k) n", p=P))\
                        .then_inc(wd_in[s], 16)
            join(sp, 7)

            for t in range(NT):
                n, dst = (P, yp[t * P:(t + 1) * P, :]) if t < NTP else (NS, ys)
                sp.wait_ge(S["y_sum"], t + 1)
                sp.dma_start(dst, x1[0:n, t, :]).then_inc(S["out_st"], 16)
            sp.wait_ge(S["out_st"], 16 * NT)

        @block.gpsimd
        def _(pool):
            c = Chain(pool, S["pool_c"])
            c.put(pool.memset(identf[:, :], 0.0))
            c.put(pool.memset(identb[:, :], 0.0))
            c.put(pool.memset(causal[:, :], 0.0))
            c.put(pool.memset(before[:, :], 1.0))
            c.put(pool.memset(q_of_row[:, :, :], 0.0))
            c.put(pool.memset(zcol[:, :], 0))
            pool.memset(onesb[:, :], 1.0)
            pool.memset(mean_of[:, :], 1.0 / CC)
            pool.memset(mhalf[:, :], -0.5)
            pool.memset(G2[:, 0, :], 0.0)
            pool.memset(glu_x[:, :, 0:TAIL], 0.0)
            c.wait()
            for m in (identf, identb):
                pool.affine_select(out=m[:, :], in_=m[:, :], compare_op=ALU.not_equal, fill=1.0, base=0,
                                   pattern=[[-1, P]], channel_multiplier=1)
            pool.affine_select(out=causal[:, :], in_=causal[:, :], compare_op=ALU.is_gt, fill=NEG, base=0,
                               pattern=[[-1, P]], channel_multiplier=1)
            pool.affine_select(out=before[:, :], in_=before[:, :], compare_op=ALU.is_gt, fill=0.0, base=0,
                               pattern=[[1, P]], channel_multiplier=-1)
            pool.affine_select(out=q_of_row[:, :, :], in_=q_of_row[:, :, :], compare_op=ALU.not_equal, fill=1.0,
                               base=0, pattern=[[0, H], [-1, DS]], channel_multiplier=1)
            for v, base, step in ((ramp_i[:, 0:MT], 0, 1), (ramp_i[:, MT:MT + EG], EG, -1),
                                  (ramp_i[:, MT + EG:MT + EG + E], E, -1), (ramp_i[:, MT + EG + E:], 0, P)):
                pool.iota(v, pattern=[[step, v.shape[1]]], base=base, channel_multiplier=0)
            pool.iota(tok_id[:, :], pattern=[[P, NT]], base=0, channel_multiplier=1).then_inc(S["pool_const"], 1)
            pool.dma_start(slot_tok_d.rearrange("(p t) a -> p (t a)", p=P), zcol[:, :]).then_inc(S["zero_idx"], 16)
            pool.wait_ge(S["zero_idx"], 16)
            join(pool, 1)

            def rstd_x(t):
                pool.wait_ge(S["x_var"], t + 1)
                pool.tensor_tensor(st[:, 2 + t % 2:3 + t % 2], st[:, t % 2:t % 2 + 1], mhalf[:, 0:1], ALU.pow)\
                    .then_inc(S["x_rstd"], 1)

            for t in range(MT_USED, MT):
                pool.dma_start(y_d[t * P:(t + 1) * P, :], G2[:, 0, :]).then_inc(S["zero_y"], 16)
            rstd_x(0)
            rstd_x(1)
            for t in range(NT):
                pool.wait_ge(S["qk_var"], t + 1)
                pool.tensor_tensor(st[:, 32:48], st[:, 16:32], mhalf[:, :], ALU.pow).then_inc(S["qk_rstd"], 1)
                pool.wait_ge(S["qk_scaled"], t + 1)
                pool.tensor_tensor(qk_t[:, t % 2, :], qk_t[:, t % 2, :], qkw, ALU.mult).then_inc(S["qk_done"], 1)
                if t + 2 < NT:
                    rstd_x(t + 2)
            pool.wait_ge(S["zero_y"], 16 * (MT - MT_USED))
            join(pool, 2)
            join(pool, 3)
            join(pool, 4)
            join(pool, 5)
            for t in range(NT):
                pool.wait_ge(S["x1_tmp"], t + 1)
                pool.wait_ge(x2_in[t % 2], 16 * (t // 2 + 1))
                n = P if t < NTP else NS
                pool.tensor_tensor(x1[0:n, t, :], x1[0:n, t, :], xt[0:n, t % 2, :], ALU.add)\
                    .then_inc(S["x1_done"], 1)
                pool.wait_ge(S["x2_var"], t + 1)
                pool.tensor_tensor(st[:, 2:3], st[:, 0:1], mhalf[:, 0:1], ALU.pow).then_inc(S["x2_rstd"], 1)
            join(pool, 6)
            pool.wait_ge(S["r_slots"], 1)
            for t in range(NT):
                n = P if t < NTP else NS
                for j in range(2):
                    pool.indirect_dma_start(
                        out=slot_tok_d, out_offset=bass.IndirectOffsetOnAxis(ap=slot_i[0:n, j, t:t + 1], axis=0),
                        in_=tok_id[0:n, t:t + 1], in_offset=None).then_inc(S["tok_st"], 16)
            pool.wait_ge(S["tok_st"], 16 * 2 * NT)
            pool.wait_ge(S["tiles_ready"], 1)
            pairs_used = pool.value_load(n_pairs[0:1, 0:1], min_val=1, max_val=MT // 2)
            slot_col = slot_tok_d.rearrange("(t p) a -> t p a", p=P)
            with pool.Fori(0, MT // 2) as i, pool.If(i < pairs_used):
                for s in range(2):
                    pool.wait_ge(S["xg_ps"], 2 * i + s + 1)
                    pool.dma_start(col_tok[:, s:s + 1],
                                   slot_col[bass.ds(2 * i + s, 1), :, :].rearrange("t p a -> (t p) a"))\
                        .then_inc(col_in[s], 16)
                    pool.wait_ge(col_in[s], 16 * i + 16)
                    settle(pool)
                    pool.indirect_dma_start(
                        out=xg[:, s, :], out_offset=None, in_=h2_d,
                        in_offset=bass.IndirectOffsetOnAxis(ap=col_tok[:, s:s + 1], axis=0)).then_inc(xg_in[s], 16)
            join(pool, 7)
            for t in range(NT):
                n = P if t < NTP else NS
                for j, buf in enumerate((ya, yb)):
                    pool.indirect_dma_start(
                        out=buf[0:n, t, :], out_offset=None, in_=y_d,
                        in_offset=bass.IndirectOffsetOnAxis(ap=slot_i[0:n, j, t:t + 1], axis=0))\
                        .then_inc(ya_in[t], 16)

        @block.scalar
        def _(act):
            act.sem_inc(S["rows_stored"], 16)
            act.wait_ge(S["const_in"], 16 * N_CONST)
            nc.scalar.activation(csig, c9, ACT.Sigmoid).then_inc(S["c_sig"], 1)
            act.wait_ge(S["cT_ps"], 1)
            nc.scalar.activation(cT[:, :, 0:1 + DB],
                                 bank[:, 0, 0:KD * 16].rearrange("p (k n) -> p k n", k=KD)[:, :, 0:1 + DB],
                                 ACT.Copy).then_inc(S["cT_sb"], 1)
            act.wait_ge(S["st_ps"], 1)
            nc.scalar.activation(cw[:, :, 0:CW + 3],
                                 bank[:, 1, 0:NCH * 64].rearrange("p (k n) -> p k n", k=NCH)[:, :, 0:CW + 3],
                                 ACT.Copy).then_inc(S["st_sb"], 1)
            for j in range(2):
                for ch in range(NCH):
                    nc.scalar.activation(
                        glu_s[:, ch, 4 * j:4 * j + 4, 0:TAIL],
                        bank[:, 4 + j, ch * 120:(ch + 1) * 120].rearrange("p (b n) -> p b n", b=4),
                        ACT.Copy).then_inc(S["st_sb"], 1)
            nc.scalar.activation(nbb[:, :], bb[:, :], ACT.Copy, scale=-1.0)
            nc.scalar.activation(nbs[:, :], bs[:, :], ACT.Copy, scale=-1.0)
            with act.Fori(0, NADA) as i:
                act.wait_ge(S["rows_done"], 2 * i + 4)
                act.dma_start(mods_d[:, bass.ds(i * D, D)], mrow).then_inc(S["rows_stored"], 16)
            join(act, 1)

            def square_x(t):
                act.wait_ge(x_in[t % 2], 16 * (t // 2 + 1))
                if t >= 2:
                    act.wait_ge(S["hT_ps"], t - 1)
                    act.wait_ge(S["x_var"], t - 1)
                nc.scalar.activation(hrow[:, t % 2, :], xt[:, t % 2, :], ACT.Square,
                                     accum_out=st[:, 4 + t % 2:5 + t % 2]).then_inc(S["x_sq"], 1)

            def evac_hT(t):
                act.wait_ge(S["hT_ps"], t + 1)
                if t >= 2:
                    act.wait_ge(S["mm_chunk"], NCHUNK * (t - 1))
                for j in range(2):
                    nc.scalar.activation(hT[:, t % 2, 4 * j:4 * j + 4, :],
                                         bank[:, 5 + j, :].rearrange("p (k n) -> p k n", k=4),
                                         ACT.Copy).then_inc(S["hT_sb"], 1)

            def evac_post(t):
                if t < NTP:
                    act.wait_ge(S["post_ps"], 3 * t + 1)
                    nc.scalar.activation(glu_x[:, :, TAIL + t * P:TAIL + (t + 1) * P],
                                         bank[:, 7, :].rearrange("p (k n) -> p k n", k=NCH), ACT.Copy)\
                        .then_inc(S["glu_sb"], 1)
                    for j, (dst, done) in enumerate(((qT_t, "q_sb"), (kT_t, "k_sb"))):
                        act.wait_ge(S["post_ps"], 3 * t + 2 + j)
                        if t >= 1:
                            act.wait_ge(S["qkT_st"], 32 * t)
                        nc.scalar.activation(dst, bank[:, 5 + j, :], ACT.Copy).then_inc(S[done], 1)
                else:
                    act.wait_ge(S["post_ps"], 3 * t + 3)
                    for ch in range(NCH):
                        nc.scalar.activation(glu_s[:, ch, :, TAIL:],
                                             bank[:, 7, ch * P:ch * P + NS].rearrange("p (b n) -> p b n", b=DB),
                                             ACT.Copy).then_inc(S["glu_sb"], 1)
                    for j, (dst, done) in enumerate(((qTs, "q_sb"), (kTs, "k_sb"))):
                        nc.scalar.activation(dst[:, :, :],
                                             bank[:, 5 + j, :].rearrange("p (k n) -> p k n", k=NPAIR)[:, :, 0:NS],
                                             ACT.Copy).then_inc(S[done], 1)

            square_x(0)
            square_x(1)
            evac_hT(0)
            for t in range(NT):
                s = t % 2
                act.wait_ge(S["mm_chunk"], NCHUNK * t + 2)
                if t >= 2:
                    act.wait_ge(S["glu_done"], t - 1)
                nc.scalar.activation(sg_t[:, s, :], bank[:, 4, :], ACT.Sigmoid).then_inc(S["sg_done"], 1)
                if t >= 1:
                    evac_post(t - 1)
                if t + 1 < NT:
                    evac_hT(t + 1)
                if t + 2 < NT:
                    square_x(t + 2)
                act.wait_ge(S["mm_chunk"], NCHUNK * t + 4)
                if t >= 1:
                    act.wait_ge(S["qk_scaled"], t)
                nc.scalar.activation(sq_t, flat[:, 0:1024], ACT.Square).then_inc(S["qk_sq"], 1)
                act.wait_ge(S["mm_chunk"], NCHUNK * t + 5)
                if t >= 2:
                    act.wait_ge(kv_st[s], 32 * (t // 2))
                nc.scalar.activation(v_t[:, s, :], bank[:, 2, :], ACT.Copy).then_inc(S["v_done"], 1)
            evac_post(NT - 1)
            join(act, 2)

            for j, (c0, n) in enumerate(LN_COLS):
                act.wait_ge(S["ln_cent"], j + 1)
                if j >= 1:
                    act.wait_ge(S["ln_done"], j)
                nc.scalar.activation(ln_a[:, :, 0:n], cvT[:, :, c0:c0 + n], ACT.Square).then_inc(S["ln_sq"], 1)
                act.wait_ge(S["ln_dv"], j + 1)
                nc.scalar.activation(ln_v[:, 0:n], ln_v[:, 0:n], ACT.Sqrt).then_inc(S["ln_std"], 1)
                act.wait_ge(S["ln_norm"], j + 1)
                for ch in range(NCH):
                    nc.scalar.activation(ln_b[:, ch, 0:n], cvT[:, ch, c0:c0 + n], ACT.Sigmoid,
                                         scale=cw[:, ch, CW + 1:CW + 2], bias=cw[:, ch, CW + 2:CW + 3])\
                        .then_inc(S["ln_sig"], 1)
            join(act, 3)

            act.sem_inc(S["sig_done"], 2)
            act.sem_inc(S["at_sb"], 2)

            def sigmoids(i, u):
                K = (u % NTP + 1) * P
                U = i * 2 * UNITS + u
                h = 4 * i + u // NTP
                act.wait_ge(S["qk_mm"], U + 1)
                act.wait_ge(S["scan_done"], U + 1)
                z = flat[:, (u % 2) * 1024:(u % 2) * 1024 + K]
                settle(act)
                nc.scalar.activation(keep[:, u % 2, 0:K], z, ACT.Sigmoid, scale=-(HD ** -0.5),
                                     bias=nbb[:, bass.ds(h, 1)]).then_inc(S["keep_done"], 1)
                act.wait_ge(S["at_ps"], U + 1)
                settle(act)
                nc.scalar.activation(sig[:, u % 2, 0:K], z, ACT.Sigmoid, scale=HD ** -0.5,
                                     bias=bb[:, bass.ds(h, 1)]).then_inc(S["sig_done"], 1)

            def evac_aT(i, u):
                K = (u % NTP + 1) * P
                U = i * 2 * UNITS + u
                act.wait_ge(S["at_ps"], U + 3)
                act.wait_ge(S["pv_mm"], U + UNITS + 1)
                nc.scalar.activation(aT[:, u % 2, 0:K], flat[:, 2048:2048 + K], ACT.Copy).then_inc(S["at_sb"], 1)

            with act.Fori(0, NPAIR // 2) as i:
                sigmoids(i, 0)
                for u in range(2 * UNITS):
                    if u + 1 < 2 * UNITS:
                        sigmoids(i, u + 1)
                    evac_aT(i, u)
            join(act, 4)

            act.sem_inc(S["s_sig"], 1)
            act.sem_inc(S["kt_act"], 1)
            act.wait_ge(S["qbd_done"], 1)
            with act.Fori(0, DB // 2) as i:
                for s in range(2):
                    b = 2 * i + s
                    act.wait_ge(S["s_mm"], b + 1)
                    settle(act)
                    nc.scalar.activation(q_stage[:, :, :], q_bd[:, bass.ds(b, 1), :, :].rearrange("p a c n -> p (a c) n"),
                                         ACT.Copy).then_inc(S["q_staged"], 1)
                    nc.scalar.activation(kT[:, :, PAST:], kTs[:, :, bass.ds(b * DS, DS)], ACT.Copy)\
                        .then_inc(S["q_staged"], 1)
                    for g in range(0, NPG, 2):
                        act.wait_ge(S["kt_ps"], NPG * b + g + 1 + 2 * NPG)
                        nc.scalar.activation(kT[:, :, g * P:(g + 1) * P],
                                             bank[:, 0, :].rearrange("p (c n) -> p c n", c=NPAIR), ACT.Copy)\
                            .then_inc(S["kt_act"], 1)
                    act.wait_ge(S["s_mm"], b + 2)
                    act.wait_ge(S["s_scan"], b + 1)
                    z = flat[0:NS, 1024:1024 + KN]
                    nc.scalar.activation(keep_s, z, ACT.Sigmoid, scale=-(HD ** -0.5), bias=nbs[:, :])\
                        .then_inc(S["s_keep"], 1)
                    act.wait_ge(S["s_at"], b + 1)
                    nc.scalar.activation(sig_s, z, ACT.Sigmoid, scale=HD ** -0.5, bias=bs[:, :])\
                        .then_inc(S["s_sig"], 1)
            join(act, 5)

            for t in range(NT):
                s = t % 2
                n = P if t < NTP else NS
                act.wait_ge(S["x1_done"], t + 1)
                if t >= 1:
                    act.wait_ge(S["x2_var"], t)
                    act.wait_ge(S["x2_sq"], t)
                nc.scalar.activation(sqx[0:n, :], x1[0:n, t, :], ACT.Square, accum_out=st[0:n, 4:5])\
                    .then_inc(S["x2_sq"], 1)
                act.wait_ge(S["h2_ps"], t + 1)
                if t >= 2:
                    act.wait_ge(S["lg_mm"], t - 1)
                for j in range(2):
                    nc.scalar.activation(h2T[:, s, 4 * j:4 * j + 4, :],
                                         bank[:, 4 + j, :].rearrange("p (k n) -> p k n", k=4), ACT.Copy)\
                        .then_inc(S["h2T_sb"], 1)
                act.wait_ge(S["lg_mm"], t + 1)
                nc.scalar.activation(logits[0:n, t, :], bank[0:n, 6, 0:E], ACT.Copy).then_inc(S["lg_sb"], 1)
            join(act, 6)
            act.wait_ge(S["r_m"], 1)
            nc.scalar.activation(r_e, r_z, ACT.Exp).then_inc(S["exp_ready"], 1)
            act.wait_ge(S["tiles_ready"], 1)
            pairs_used = act.value_load(n_pairs[0:1, 0:1], min_val=1, max_val=MT // 2)

            act.sem_inc(S["xgT_sb"], 1)
            act.sem_inc(S["g_sig"], 2)
            act.sem_inc(S["y_lo"], 1)

            def swish_gate(i, s):
                t = 2 * i + s
                act.wait_ge(S["gu_mm"], t + 3)
                act.wait_ge(S["aT_ps"], t + 1)
                nc.scalar.activation(act_t[:, s, :], bank[:, 2 * s, :], ACT.Sigmoid).then_inc(S["g_sig"], 1)

            def out_lo(i, s):
                t = 2 * i + s
                act.wait_ge(S["y_mm"], 2 * t + 5)
                act.wait_ge(y_st[s], 16 * i + 16)
                nc.scalar.activation(y_t[:, s, 0:512], bank[:, 6, :], ACT.Copy).then_inc(S["y_lo"], 1)
                act.wait_ge(S["y_lo"], t + 2)
                act.wait_ge(S["y_hi"], t + 2)
                act.dma_start(y_d[bass.ds(t * P, P), :], y_t[:, s, :]).then_inc(y_st[s], 16)

            for s in range(2):
                act.sem_inc(y_st[s], 16)
            with act.Fori(0, MT // 2) as i, act.If(i < pairs_used):
                for s in range(2):
                    t = 2 * i + s
                    act.wait_ge(S["xg_ps"], t + 3)
                    act.wait_ge(S["gu_mm"], t + 1)
                    nc.scalar.activation(xgT[:, s, 0:4, :],
                                         bank[:, 4, :].rearrange("p (k n) -> p k n", k=4), ACT.Copy)\
                        .then_inc(S["xgT_sb"], 1)
                    swish_gate(i, s)
                out_lo(i, 0)
                out_lo(i, 1)
            for s in range(2):
                act.wait_ge(y_st[s], 16 * pairs_used + 16)
            settle(act)
            join(act, 7)

            for t in range(NT):
                n = P if t < NTP else NS
                act.wait_ge(ya_in[t], 32)
                nc.scalar.activation(ya[0:n, t, :], ya[0:n, t, :], ACT.Copy, scale=wgt[0:n, 0, t:t + 1])\
                    .then_inc(S["y_first"], 1)

        @block.tensor
        def _(pe):
            pe.sem_inc(S["ada_used"], 4)
            pe.wait_ge(S["pool_const"], 1)
            pe.wait_ge(S["c_silu"], 1)
            for k in range(KD):
                mm = pe.transpose(bank[:, 0, k * 16:k * 16 + 1 + DB], c9[:, k * P:(k + 1) * P],
                                  identf[0:1 + DB, 0:1 + DB])
            mm.then_inc(S["cT_ps"], 1)
            for ch in range(NCH):
                pe.transpose(bank[:, 1, ch * 64:ch * 64 + CW + 3], xt[0:CW + 3, 0, ch * P:(ch + 1) * P],
                             identf[0:CW + 3, 0:CW + 3])
            for j in range(2):
                for ch in range(NCH):
                    mm = pe.transpose(bank[:, 4 + j, ch * 120:(ch + 1) * 120],
                                      xt[0:120, 1, j * CC + ch * P:j * CC + (ch + 1) * P], identf[0:120, 0:120])
            mm.then_inc(S["st_ps"], 1)
            pe.wait_ge(S["cT_sb"], 1)
            with pe.Fori(0, NADA) as i:
                for cc in range(2):
                    pe.wait_ge(S["rows_done"], 2 * i + cc + 1)
                    for k in range(KD):
                        s = 2 * cc + k // 4
                        if k % 4 == 0:
                            pe.wait_ge(ada_in[s], 16 * i + 16)
                        mm = pe.matmul(bank[0:1 + DB, 2 + cc, :], cT[:, k, 0:1 + DB], ada[:, s, k % 4, :],
                                       start=(k == 0), stop=(k == KD - 1))
                        if k % 4 == 3:
                            mm.then_inc(S["ada_used"], 1)
            join(pe, 1)

            def turn_h(t):
                pe.wait_ge(S["h_ready"], t + 1)
                if t >= 1:
                    pe.wait_ge(S["hT_sb"], 2 * t)
                if t >= 2:
                    pe.wait_ge(S["q_sb"], t - 1)
                    pe.wait_ge(S["k_sb"], t - 1)
                for k in range(KD):
                    mm = pe.transpose(bank[:, 5 + k // 4, (k % 4) * P:(k % 4 + 1) * P],
                                      hrow[:, t % 2, k * P:(k + 1) * P], identf[:, :])
                mm.then_inc(S["hT_ps"], 1)

            def turn_post(t):
                s = t % 2
                pe.wait_ge(S["glu_done"], t + 1)
                if t >= 1:
                    pe.wait_ge(S["glu_sb"], t)
                for ch in range(NCH):
                    mm = pe.transpose(bank[:, 7, ch * P:(ch + 1) * P], glu_t[:, s, ch * P:(ch + 1) * P], identf[:, :])
                mm.then_inc(S["post_ps"], 1)
                pe.wait_ge(S["qk_done"], t + 1)
                pe.wait_ge(S["hT_sb"], min(2 * (t + 2), 2 * NT))
                for j in range(2):
                    for p in range(NPAIR):
                        mm = pe.transpose(bank[:, 5 + j, p * P:(p + 1) * P],
                                          qk_t[:, s, j * AW + p * P:j * AW + (p + 1) * P], identf[:, :])
                    mm.then_inc(S["post_ps"], 1)

            turn_h(0)
            for t in range(NT):
                s = t % 2
                if t == 0:
                    pe.wait_ge(S["w_in_in"], 16 * KD)
                pe.wait_ge(S["hT_sb"], 2 * (t + 1))
                for n, (cc, freed) in enumerate(((3, "glu_done"), (4, "glu_done"), (0, "qk_scaled"),
                                                 (1, "qk_scaled"), (2, "v_done"))):
                    if t >= 1:
                        pe.wait_ge(S[freed], t)
                        if cc < 2:
                            pe.wait_ge(S["qk_sq"], t)
                        if cc == 4:
                            pe.wait_ge(S["sg_done"], t)
                    for k in range(KD):
                        mm = pe.matmul(bank[:, cc, :], hT[:, s, k, :], w_in_sb[:, k, cc * 512:(cc + 1) * 512],
                                       start=(k == 0), stop=(k == KD - 1))
                    mm.then_inc(S["mm_chunk"], 1)
                    if n == 1 and t >= 1:
                        turn_post(t - 1)
                    if n == 2 and t + 1 < NT:
                        turn_h(t + 1)
            turn_post(NT - 1)
            join(pe, 2)

            for j, (c0, n) in enumerate(LN_COLS):
                if j == 0:
                    pe.wait_ge(S["conv_done"], 1)
                if j >= 1:
                    pe.wait_ge(S["ln_cent"], j)
                    pe.wait_ge(S["ln_dv"], j)
                for ch in range(NCH):
                    mm = pe.matmul(bank[:, 0, 0:n], mean_of[:, :], cvT[:, ch, c0:c0 + n],
                                   start=(ch == 0), stop=(ch == NCH - 1))
                mm.then_inc(S["ln_mean"], 1)
                pe.wait_ge(S["ln_sq"], j + 1)
                for ch in range(NCH):
                    mm = pe.matmul(bank[:, 1, 0:n], mean_of[:, :], ln_a[:, ch, 0:n],
                                   start=(ch == 0), stop=(ch == NCH - 1))
                mm.then_inc(S["ln_var"], 1)
            join(pe, 3)

            pe.sem_inc(S["at_ps"], 2)
            pe.sem_inc(S["pv_mm"], 2 + UNITS)

            def scores(i, u):
                s, hh, qb = u // UNITS, (u // NTP) % 2, u % NTP
                U = i * 2 * UNITS + u
                if u % UNITS == 0:
                    pe.wait_ge(stage_in[s], 48 * i + 48)
                pe.wait_ge(S["sig_done"], U + 1)
                K = (qb + 1) * P
                pp = slice(64 * hh, 64 * hh + 64)
                for c0 in range(0, K, 512):
                    n = min(512, K - c0)
                    last = c0 + n == K
                    mm = pe.matmul(bank[:, 2 * (u % 2) + c0 // 512, 0:n], stage[pp, s, 0, qb * P:(qb + 1) * P],
                                   stage[pp, s, 1, c0:c0 + n], start=True, stop=not last)
                k0 = qb * P % 512
                mm = pe.matmul(bank[:, 2 * (u % 2) + qb // 4, k0:k0 + P], identb[:, :], causal[:, :],
                               start=False, stop=True)
                mm.then_inc(S["qk_mm"], 1)

            def turn_a(i, u):
                U = i * 2 * UNITS + u
                pe.wait_ge(S["a_done"], U + 1)
                pe.wait_ge(S["at_sb"], U + 2)
                for kb in range(u % NTP + 1):
                    mm = pe.transpose(bank[:, 4 + kb // 4, (kb % 4) * P:(kb % 4 + 1) * P],
                                      sig[:, u % 2, kb * P:(kb + 1) * P], identf[:, :])
                mm.then_inc(S["at_ps"], 1)

            def values(i, u):
                s, hh, qb = u // UNITS, (u // NTP) % 2, u % NTP
                U = i * 2 * UNITS + u
                pe.wait_ge(S["at_sb"], U + 3)
                if u % 4 == 0:
                    pe.wait_ge(S["o_sb"], i * (2 * UNITS // 4) + u // 4 + 1)
                ob = bank[64 * hh:64 * hh + 64, 6 + (u // 4) % 2, (qb % 4) * P:(qb % 4 + 1) * P]
                for kb in range(qb + 1):
                    mm = pe.matmul(ob, stage[:, s, 2, kb * P + 64 * hh:kb * P + 64 * hh + 64],
                                   aT[:, u % 2, kb * P:(kb + 1) * P], start=(kb == 0), stop=(kb == qb))
                mm.then_inc(S["pv_mm"], 1)

            with pe.Fori(0, NPAIR // 2) as i:
                scores(i, 0)
                for u in range(2 * UNITS):
                    if u + 1 < 2 * UNITS:
                        scores(i, u + 1)
                    turn_a(i, u)
                    if u >= 1:
                        values(i, u - 1)
                values(i, 2 * UNITS - 1)
            join(pe, 4)

            pe.sem_inc(S["kt_ps"], 2 * NPG)
            pe.sem_inc(S["s_pv"], 2)
            pe.sem_inc(S["s_mm"], 1)
            pe.sem_inc(S["s_at"], 1)

            def turn_keys(i, s):
                b = 2 * i + s
                pe.wait_ge(k_in[s], 16 * NPG * i + 16 * NPG)
                for g in range(NPG):
                    pe.wait_ge(S["kt_act" if g % 2 == 0 else "kt_dve"], 4 * b + g // 2 + 1)
                    for p in range(NPAIR):
                        mm = pe.transpose(bank[:, g % 2, p * P:(p + 1) * P], k_pg[:, s, g, p * P:(p + 1) * P],
                                          identf[:, :])
                    mm.then_inc(S["kt_ps"], 1)

            def scores_s(i, s):
                b = 2 * i + s
                pe.wait_ge(S["kt_act"], 4 * b + 5)
                pe.wait_ge(S["kt_dve"], 4 * b + 5)
                pe.wait_ge(S["q_staged"], 2 * b + 2)
                pe.wait_ge(S["s_sig"], b + 1)
                for c0 in range(0, KN, 512):
                    n = min(512, KN - c0)
                    for p in range(NPAIR):
                        pe.matmul(bank[0:NS, 2 + c0 // 512, 0:n], q_stage[:, p, :], kT[:, p, c0:c0 + n],
                                  start=(p == 0), stop=(p == NPAIR - 1 and n == 512))
                mm = pe.matmul(bank[0:NS, 4, 0:DS], q_of_row[:, :, :].rearrange("p h i -> p (h i)"),
                               causal[0:DS, 0:DS], start=False, stop=True)
                mm.then_inc(S["s_mm"], 1)

            def turn_a_s(i, s):
                b = 2 * i + s
                pe.wait_ge(S["s_a"], b + 1)
                pe.wait_ge(S["s_at_sb"], 2 * b + 1)
                settle(pe)
                for g in range(NPG):
                    pe.transpose(bank[:, 5, g * NS:(g + 1) * NS], sig_s[:, g * P:(g + 1) * P], identf[0:NS, 0:NS])
                pe.transpose(bank[0:DS, 5, NPG * NS:(NPG + 1) * NS], sig_s[:, PAST:PAST + DS], identf[0:NS, 0:NS])\
                    .then_inc(S["s_at"], 1)

            def values_s(i, s):
                b = 2 * i + s
                pe.wait_ge(v_in[s], 16 * (NPG + 1) * i + 16 * (NPG + 1))
                pe.wait_ge(S["s_at_sb"], 2 * b + 3)
                pe.wait_ge(S["s_o"], 2 * b + 1)
                for p in range(NPAIR):
                    for g in range(NPG):
                        pe.matmul(bank[:, 6, p * 8:p * 8 + 8], v_pg[:, s, g, p * P:(p + 1) * P],
                                  aT_s[:, g, p * 8:p * 8 + 8], start=(g == 0), stop=False)
                    mm = pe.matmul(bank[:, 6, p * 8:p * 8 + 8], v_new[:, s, p * P:(p + 1) * P],
                                   aT_s[0:DS, NPG, p * 8:p * 8 + 8], start=False, stop=True)
                mm.then_inc(S["s_pv"], 1)

            with pe.Fori(0, DB // 2) as i:
                turn_keys(i, 0)
                scores_s(i, 0)
                turn_keys(i, 1)
                turn_a_s(i, 0)
                values_s(i, 0)
                scores_s(i, 1)
                turn_a_s(i, 1)
                values_s(i, 1)
            join(pe, 5)

            pe.wait_ge(S["w_out_in"], 16 * KD)

            def mix(t):
                n = P if t < NTP else NS
                if t >= 2:
                    pe.wait_ge(S["x1_tmp"], t - 1)
                for cc in range(2):
                    for k in range(KD):
                        cat = oT if k < NPAIR else cvT
                        mm = pe.matmul(bank[0:n, 2 * (t % 2) + cc, :], cat[:, k % NPAIR, t * P:t * P + n],
                                       w_out_sb[:, k, cc * 512:(cc + 1) * 512], start=(k == 0), stop=(k == KD - 1))
                mm.then_inc(S["mix_mm"], 1)

            def route(t):
                n = P if t < NTP else NS
                pe.wait_ge(S["h2_done"], t + 1)
                if t >= 1:
                    pe.wait_ge(S["h2T_sb"], 2 * t)
                for k in range(KD):
                    mm = pe.transpose(bank[:, 4 + k // 4, (k % 4) * P:(k % 4) * P + n],
                                      h2[0:n, t % 2, k * P:(k + 1) * P], identf[0:n, 0:n])
                mm.then_inc(S["h2_ps"], 1)

            def router(t):
                n = P if t < NTP else NS
                pe.wait_ge(S["h2T_sb"], 2 * t + 2)
                if t >= 1:
                    pe.wait_ge(S["lg_sb"], t)
                for k in range(KD):
                    mm = pe.matmul(bank[0:n, 6, 0:E], h2T[:, t % 2, k, 0:n], wr[:, k, :],
                                   start=(k == 0), stop=(k == KD - 1))
                mm.then_inc(S["lg_mm"], 1)

            mix(0)
            for t in range(NT):
                if t + 1 < NT:
                    mix(t + 1)
                route(t)
                router(t)
            join(pe, 6)
            pe.wait_ge(S["r_pos"], 1)
            pe.matmul(bank[:, 0, 0:NT * E], before[:, :], r_maskb, start=True, stop=True)
            pe.matmul(bank[:, 1, 0:NT * E], onesb[:, :], r_maskb, start=True, stop=True).then_inc(S["r_m"], 1)
            pe.wait_ge(S["tiles_ready"], 1)
            pairs_used = pe.value_load(n_pairs[0:1, 0:1], min_val=1, max_val=MT // 2)

            pe.sem_inc(S["gu_mm"], 2)
            pe.sem_inc(S["y_mm"], 4)
            pe.sem_inc(S["xg_ps"], 2)
            pe.sem_inc(S["aT_ps"], 2)

            def turn_x(i, s):
                t = 2 * i + s
                pe.wait_ge(xg_in[s], 16 * i + 16)
                pe.wait_ge(S["xgT_sb"], t + 1)
                pe.wait_ge(S["xgT_hi"], t + 1)
                pe.wait_ge(S["aT_sb"], 2 * i + 1)
                for k in range(KD):
                    mm = pe.transpose(bank[:, 4 + k // 4, (k % 4) * P:(k % 4 + 1) * P],
                                      xg[:, s, k * P:(k + 1) * P], identf[:, :])
                mm.then_inc(S["xg_ps"], 1)

            def gate_or_up(i, s, w):
                t = 2 * i + s
                if w == 0:
                    pe.wait_ge(S["xgT_sb"], t + 2)
                    pe.wait_ge(S["xgT_hi"], t + 2)
                    pe.wait_ge(S["g_sig"], t + 1)
                    pe.wait_ge(S["act_done"], t + 1)
                w_sb, arrived = ((wg_sb, wg_in), (wu_sb, wu_in))[w]
                pe.wait_ge(arrived[s], 16 * i + 16)
                for k in range(KD):
                    mm = pe.matmul(bank[:, 2 * s + w, :], xgT[:, s, k, :], w_sb[:, s, k, :],
                                   start=(k == 0), stop=(k == KD - 1))
                if w == 1:
                    mm.then_inc(S["gu_mm"], 1)

            def turn_act(i, s):
                t = 2 * i + s
                pe.wait_ge(S["act_done"], t + 3)
                pe.wait_ge(S["aT_sb"], t + 1)
                for k in range(KF):
                    mm = pe.transpose(bank[:, 4, k * P:(k + 1) * P], act_t[:, s, k * P:(k + 1) * P], identf[:, :])
                mm.then_inc(S["aT_ps"], 1)

            def down(i, s, w):
                t = 2 * i + s
                if w == 0:
                    pe.wait_ge(S["aT_sb"], t + 2)
                    pe.wait_ge(wd_in[s], 16 * i + 16)
                pe.wait_ge(S["y_lo" if w == 0 else "y_hi"], t + 1)
                for k in range(KF):
                    mm = pe.matmul(bank[:, 6 + w, :], actT[:, s, k, :], wd_sb[:, s, k, w * 512:(w + 1) * 512],
                                   start=(k == 0), stop=(k == KF - 1))
                mm.then_inc(S["y_mm"], 1)

            with pe.Fori(0, MT // 2) as i, pe.If(i < pairs_used):
                turn_x(i, 0)
                gate_or_up(i, 0, 0)
                gate_or_up(i, 0, 1)
                turn_x(i, 1)
                gate_or_up(i, 1, 0)
                turn_act(i, 0)
                gate_or_up(i, 1, 1)
                down(i, 0, 0)
                turn_act(i, 1)
                down(i, 0, 1)
                down(i, 1, 0)
                down(i, 1, 1)
            join(pe, 7)

        @block.vector
        def _(dve):
            c = Chain(dve, S["dve_c"])
            V = nc.vector
            dve.sem_inc(S["rows_done"], 2)
            dve.wait_ge(S["c_sig"], 1)
            V.tensor_tensor(c9, c9, csig, ALU.mult).then_inc(S["c_silu"], 1)
            with dve.Fori(0, NADA) as i:
                for cc in range(2):
                    dve.wait_ge(S["ada_used"], 4 * i + 2 * cc + 6)
                    dve.wait_ge(S["brow_in"], 16 * i + 16)
                    dve.wait_ge(S["rows_stored"], 16 * i + 16)
                    V.tensor_tensor(mrow[:, cc * 512:(cc + 1) * 512], bank[0:1 + DB, 2 + cc, :],
                                    brow[:, cc * 512:(cc + 1) * 512], ALU.add).then_inc(S["rows_done"], 1)
            dve.wait_ge(S["mod1_in"], 16 * 7)
            for kind, n in ((0, P), (1, NS)):
                c.put(V.scalar_tensor_tensor(AB[0:n, kind, 0, :], AB[0:n, kind, 0, :], 1.0, hrow[0:n, 0, :],
                                             ALU.add, ALU.mult))
            c.wait()
            join(dve, 1)

            def var_x(t):
                dve.wait_ge(S["x_sq"], t + 1)
                s = t % 2
                if t >= 2:
                    dve.wait_ge(S["x_rstd"], t - 1)
                V.tensor_scalar(st[:, s:s + 1], st[:, 4 + s:5 + s], 1.0 / D, EPS, ALU.mult, ALU.add)\
                    .then_inc(S["x_var"], 1)

            def norm_x(t):
                s = t % 2
                n, kind = (P, 0) if t < NTP else (NS, 1)
                dve.wait_ge(S["x_rstd"], t + 1)
                c.put(V.scalar_tensor_tensor(hrow[0:n, s, :], xt[0:n, s, :], st[0:n, 2 + s:3 + s],
                                             AB[0:n, kind, 0, :], ALU.mult, ALU.mult))
                c.wait()
                V.tensor_tensor(hrow[0:n, s, :], hrow[0:n, s, :], AB[0:n, kind, 1, :], ALU.add)\
                    .then_inc(S["h_ready"], 1)

            def conv_taps(pair, chs, t0, t1):
                n0 = pair * 2 * P
                if t0 == 0:
                    dve.wait_ge(S["glu_sb"], 2 * pair + 2)
                for tap in range(t0, t1):
                    for ch in chs:
                        out = cvT[:, ch, n0:n0 + 2 * P]
                        src = glu_x[:, ch, n0 + tap:n0 + tap + 2 * P]
                        if tap == 0:
                            c.put(V.tensor_scalar(out, src, cw[:, ch, 0:1], cw[:, ch, CW:CW + 1], ALU.mult, ALU.add))
                        else:
                            c.wait(back=len(chs) - 1)
                            c.put(V.scalar_tensor_tensor(out, src, cw[:, ch, tap:tap + 1], out, ALU.mult, ALU.add))

            def conv_part(t, part):
                j = t - 3
                if j >= 0:
                    chs = (0, 1) if j % 2 == 0 else (2, 3)
                    conv_taps(j // 2, chs, (0, 8, 16, 24)[part], (8, 16, 24, CW)[part])

            dve.wait_ge(S["st_sb"], 1)
            var_x(0)
            norm_x(0)
            var_x(1)
            norm_x(1)
            for t in range(NT):
                s = t % 2
                dve.wait_ge(S["sg_done"], t + 1)
                dve.wait_ge(S["mm_chunk"], NCHUNK * t + 2)
                if t >= 2:
                    dve.wait_ge(S["post_ps"], 3 * (t - 2) + 1)
                if t == NTP + 1:
                    dve.wait_ge(S["conv_st"], 16)
                V.tensor_tensor(glu_t[:, s, :], bank[:, 3, :], sg_t[:, s, :], ALU.mult).then_inc(S["glu_done"], 1)
                conv_part(t, 0)
                dve.wait_ge(S["qk_sq"], t + 1)
                c.wait()
                c.put(V.tensor_reduce(st[:, 48:64], sq_t.rearrange("p (h d) -> p h d", d=HD), AX_X, ALU.add))
                c.wait()
                if t >= 1:
                    dve.wait_ge(S["qk_rstd"], t)
                V.tensor_scalar(st[:, 16:32], st[:, 48:64], 1.0 / HD, EPS, ALU.mult, ALU.add)\
                    .then_inc(S["qk_var"], 1)
                conv_part(t, 1)
                dve.wait_ge(S["qk_rstd"], t + 1)
                if t >= 2:
                    dve.wait_ge(S["post_ps"], 3 * (t - 2) + 3)
                    dve.wait_ge(kv_st[s], 32 * (t // 2))
                V.tensor_tensor(qk_t[:, s, :].rearrange("p (h d) -> p h d", d=HD),
                                flat[:, 0:1024].rearrange("p (h d) -> p h d", d=HD),
                                st[:, 32:48].unsqueeze(2).broadcast_to([P, 16, HD]), ALU.mult)\
                    .then_inc(S["qk_scaled"], 1)
                conv_part(t, 2)
                if t + 2 < NT:
                    var_x(t + 2)
                    norm_x(t + 2)
                conv_part(t, 3)
            conv_taps(3, (0, 1, 2, 3), 0, CW)
            dve.wait_ge(S["glu_sb"], NTP + NCH)
            dve.wait_ge(S["st_sb"], 9)
            for tap in range(CW):
                for ch in range(NCH):
                    out = cvT[:, ch, SEQ:TOK].rearrange("p (b n) -> p b n", b=DB)
                    src = glu_s[:, ch, :, tap:tap + DS]
                    if tap == 0:
                        c.put(V.tensor_scalar(out, src, cw[:, ch, 0:1], cw[:, ch, CW:CW + 1], ALU.mult, ALU.add))
                    else:
                        c.wait(back=NCH - 1)
                        c.put(V.scalar_tensor_tensor(out, src, cw[:, ch, tap:tap + 1], out, ALU.mult, ALU.add))
            c.wait()
            join(dve, 2)

            dve.sem_inc(S["conv_done"], 1)
            for j, (c0, n) in enumerate(LN_COLS):
                y = cvT[:, :, c0:c0 + n]
                dve.wait_ge(S["ln_mean"], j + 1)
                V.tensor_tensor(y, y, bank[:, 0, 0:n].unsqueeze(1).broadcast_to([P, NCH, n]), ALU.subtract)\
                    .then_inc(S["ln_cent"], 1)
                dve.wait_ge(S["ln_var"], j + 1)
                V.tensor_scalar(ln_v[:, 0:n], bank[:, 1, 0:n], EPS, None, ALU.add).then_inc(S["ln_dv"], 1)
                dve.wait_ge(S["ln_std"], j + 1)
                c.put(V.reciprocal(ln_r[:, 0:n], ln_v[:, 0:n]))
                c.wait()
                dve.wait_ge(S["ln_cent"], j + 1)
                V.tensor_tensor(y, y, ln_r[:, 0:n].unsqueeze(1).broadcast_to([P, NCH, n]), ALU.mult)\
                    .then_inc(S["ln_norm"], 1)
                dve.wait_ge(S["ln_norm"], j + 1)
                dve.wait_ge(S["ln_sig"], NCH * (j + 1))
                for ch in range(NCH):
                    c.put(V.tensor_scalar(cvT[:, ch, c0:c0 + n], cvT[:, ch, c0:c0 + n], cw[:, ch, CW + 1:CW + 2],
                                          cw[:, ch, CW + 2:CW + 3], ALU.mult, ALU.add))
                c.wait()
                V.tensor_tensor(y, y, ln_b[:, :, 0:n], ALU.mult).then_inc(S["ln_done"], 1)
            join(dve, 3)

            dve.sem_inc(S["scan_done"], 2)
            dve.sem_inc(S["o_sb"], 2)
            for s in range(2):
                c.put(V.memset(prod[:, s, 1024:1025], 1.0))
            c.wait()

            def stick(i, u):
                K = (u % NTP + 1) * P
                U = i * 2 * UNITS + u
                dve.wait_ge(S["keep_done"], U + 1)
                kept = prod[:, u % 2, 1024 - K:1024]
                V.tensor_tensor_scan(kept[:, ::-1], keep[:, u % 2, 0:K][:, ::-1], keep[:, u % 2, 0:K][:, ::-1],
                                     1.0, ALU.mult, ALU.bypass).then_inc(S["scan_done"], 1)
                dve.wait_ge(S["sig_done"], U + 3)
                dve.wait_ge(S["scan_done"], U + 3)
                V.tensor_tensor(sig[:, u % 2, 0:K], sig[:, u % 2, 0:K], prod[:, u % 2, 1025 - K:1025], ALU.mult)\
                    .then_inc(S["a_done"], 1)

            def evac_o(i, g):
                pair = 2 * i + g // 4
                hh, half = (g // 2) % 2, g % 2
                dve.wait_ge(S["pv_mm"], i * 2 * UNITS + 4 * g + 4 + 2 + UNITS)
                pp = slice(64 * hh, 64 * hh + 64)
                V.tensor_copy(oT[pp, bass.ds(pair, 1), half * 512:(half + 1) * 512].rearrange("p a n -> p (a n)"),
                              bank[pp, 6 + g % 2, :]).then_inc(S["o_sb"], 1)

            with dve.Fori(0, NPAIR // 2) as i:
                for u in range(2 * UNITS):
                    stick(i, u)
                    if u >= 5 and (u - 5) % 4 == 0:
                        evac_o(i, (u - 5) // 4)
                evac_o(i, 2 * UNITS // 4 - 1)
            join(dve, 4)

            dve.sem_inc(S["kt_dve"], 1)
            dve.sem_inc(S["s_scan"], 1)
            dve.sem_inc(S["s_at_sb"], 1)
            dve.sem_inc(S["s_o"], 1)
            c.put(V.memset(xt[:, 0, :], 0.0))
            c.put(V.memset(prod_s[:, KN:KN + 1], 1.0))
            c.wait()
            for h in range(H):
                pp = slice(64 * (h % 2), 64 * (h % 2) + 64)
                c.put(V.tensor_copy(q_bd[pp, :, h // 2, h * DS:(h + 1) * DS],
                                    qTs[pp, h // 2, :].rearrange("p (b n) -> p b n", b=DB)))
            c.wait()
            dve.sem_inc(S["qbd_done"], 1)
            with dve.Fori(0, DB // 2) as i:
                def keys_odd(s):
                    b = 2 * i + s
                    dve.wait_ge(S["s_mm"], b + 1)
                    for g in range(1, NPG, 2):
                        dve.wait_ge(S["kt_ps"], NPG * b + g + 1 + 2 * NPG)
                        V.tensor_copy(kT[:, :, g * P:(g + 1) * P],
                                      bank[:, 1, :].rearrange("p (c n) -> p c n", c=NPAIR)).then_inc(S["kt_dve"], 1)

                def stick_s(s):
                    b = 2 * i + s
                    dve.wait_ge(S["s_keep"], b + 1)
                    V.tensor_tensor_scan(prod_s[:, 0:KN][:, ::-1], keep_s[:, ::-1], keep_s[:, ::-1], 1.0,
                                         ALU.mult, ALU.bypass).then_inc(S["s_scan"], 1)
                    dve.wait_ge(S["s_scan"], b + 2)
                    dve.wait_ge(S["s_sig"], b + 2)
                    V.tensor_tensor(sig_s, sig_s, prod_s[:, 1:KN + 1], ALU.mult).then_inc(S["s_a"], 1)

                def out_s(s):
                    b = 2 * i + s
                    dve.wait_ge(S["s_at"], b + 2)
                    dve.wait_ge(S["s_pv"], b + 2)
                    V.tensor_copy(aT_s[:, 0:NPG, :], bank[:, 5, 0:NPG * NS].rearrange("p (g n) -> p g n", g=NPG))\
                        .then_inc(S["s_at_sb"], 1)
                    V.tensor_copy(aT_s[0:DS, NPG, :], bank[0:DS, 5, NPG * NS:(NPG + 1) * NS])\
                        .then_inc(S["s_at_sb"], 1)
                    dve.wait_ge(S["s_pv"], b + 3)
                    for hh in range(2):
                        pp = slice(64 * hh, 64 * hh + 64)
                        V.tensor_copy(oT[pp, :, bass.ds(b * DS + SEQ, DS)],
                                      bank[pp, 6, 0:32].rearrange("p (c n) -> p c n", c=NPAIR)[:, :, 4 * hh:4 * hh + 4])\
                            .then_inc(S["s_o"], 1)

                keys_odd(0)
                stick_s(0)
                keys_odd(1)
                out_s(0)
                stick_s(1)
                out_s(1)
            join(dve, 5)

            dve.wait_ge(S["mod2_in"], 16 * 9)
            for kind, n in ((0, P), (1, NS)):
                c.put(V.scalar_tensor_tensor(mod2[0:n, 1, kind, :], mod2[0:n, 1, kind, :], 1.0, gffn[0:n, :],
                                             ALU.add, ALU.mult))
            c.put(V.memset(logits[:, NTP, :], 0.0))
            c.wait()
            dve.sem_inc(S["mod2_done"], 1)

            def gated(t):
                n, kind = (P, 0) if t < NTP else (NS, 1)
                dve.wait_ge(S["mix_mm"], t + 1)
                b0 = 1024 * (t % 2)
                V.tensor_tensor(x1[0:n, t, :], flat[0:n, b0:b0 + D], mod2[0:n, 0, kind, :], ALU.mult)\
                    .then_inc(S["x1_tmp"], 1)

            gated(0)
            for t in range(NT):
                s = t % 2
                n, kind = (P, 0) if t < NTP else (NS, 1)
                dve.wait_ge(S["x2_sq"], t + 1)
                if t >= 1:
                    dve.wait_ge(S["x2_rstd"], t)
                V.tensor_scalar(st[0:n, 0:1], st[0:n, 4:5], 1.0 / D, EPS, ALU.mult, ALU.add).then_inc(S["x2_var"], 1)
                dve.wait_ge(S["x2_rstd"], t + 1)
                if t >= 2:
                    dve.wait_ge(S["h2_ps"], t - 1)
                    dve.wait_ge(h2_stored[s], 16 * (t // 2))
                c.put(V.scalar_tensor_tensor(h2[0:n, s, :], x1[0:n, t, :], st[0:n, 2:3], mod2[0:n, 1, kind, :],
                                             ALU.mult, ALU.mult))
                c.wait()
                V.tensor_tensor(h2[0:n, s, :], h2[0:n, s, :], mod2[0:n, 2, kind, :], ALU.add)\
                    .then_inc(S["h2_done"], 1)
                if t + 1 < NT:
                    gated(t + 1)
            join(dve, 6)

            def op(ins):
                c.put(ins)
                c.wait()

            def col(v, n):
                return v.unsqueeze(2).broadcast_to([P, NT, n])

            def row(v, n, m):
                return v.unsqueeze(1).broadcast_to([P, n, m])

            op(V.tensor_copy(ramp[:, :], ramp_i[:, :]))
            op(V.tensor_reduce(r_a, logits[:, :, :], AX_X, ALU.max))
            op(V.tensor_tensor(r_z, logits[:, :, :], col(r_a, E), ALU.subtract))
            dve.sem_inc(S["r_m"], 1)
            dve.wait_ge(S["exp_ready"], 1)
            op(V.tensor_reduce(r_a, r_e, AX_X, ALU.add))
            op(V.reciprocal(r_b, r_a))
            op(V.tensor_tensor(r_p, r_e, col(r_b, E), ALU.mult))
            op(V.tensor_tensor(r_sel, r_p, row(br[:, :], NT, E), ALU.add))
            pairs = r_sel.rearrange("p t (g j) -> p (t g) j", j=2)
            op(V.tensor_tensor(r_hi, pairs[:, :, 0], pairs[:, :, 1], ALU.max))
            op(V.tensor_tensor(r_lo, pairs[:, :, 0], pairs[:, :, 1], ALU.min))
            hi2 = r_hi.rearrange("p (g j) -> p g j", j=2)
            lo2 = r_lo.rearrange("p (g j) -> p g j", j=2)
            op(V.tensor_tensor(r_gs, hi2[:, :, 0], hi2[:, :, 1], ALU.add))
            for j in range(2):
                op(V.tensor_tensor(r_g1, hi2[:, :, j], lo2[:, :, j], ALU.add))
                op(V.tensor_tensor(r_gs, r_gs, r_g1, ALU.max))
            gs = r_gs.rearrange("p (t g) -> p t g", g=EG)
            g1 = r_g1.rearrange("p (t g) -> p t g", g=EG)
            op(V.tensor_reduce(r_a, gs, AX_X, ALU.max))
            op(V.tensor_tensor(g1, gs, col(r_a, EG), ALU.is_equal))
            op(V.tensor_tensor(g1, g1, row(g_rank, NT, EG), ALU.mult))
            op(V.tensor_reduce(r_a, g1, AX_X, ALU.max))
            op(V.tensor_tensor(g1, g1, col(r_a, EG), ALU.is_equal))
            in_grp = r_g1.unsqueeze(2).broadcast_to([P, NT * EG, EPG])
            sel4 = r_sel.rearrange("p t (g j) -> p (t g) j", j=EPG)
            off4 = r_off.rearrange("p t (g j) -> p (t g) j", j=EPG)
            op(V.tensor_tensor(sel4, sel4, in_grp, ALU.mult))
            op(V.tensor_scalar(off4, in_grp, -NEG, NEG, ALU.mult, ALU.add))
            op(V.tensor_tensor(r_sel, r_sel, r_off, ALU.add))
            for j, hot in enumerate((r_h0, r_h1)):
                op(V.tensor_reduce(r_a, r_sel, AX_X, ALU.max))
                op(V.tensor_tensor(hot, r_sel, col(r_a, E), ALU.is_equal))
                op(V.tensor_tensor(hot, hot, row(e_rank, NT, E), ALU.mult))
                op(V.tensor_reduce(r_a, hot, AX_X, ALU.max))
                op(V.tensor_tensor(hot, hot, col(r_a, E), ALU.is_equal))
                op(V.tensor_tensor(r_off, r_p, hot, ALU.mult))
                op(V.tensor_reduce(wgt[:, j, :], r_off, AX_X, ALU.add))
                if j == 0:
                    op(V.tensor_scalar(r_off, hot, 3.0 * NEG, None, ALU.mult))
                    op(V.tensor_tensor(r_sel, r_sel, r_off, ALU.add))
            op(V.tensor_tensor(r_a, wgt[:, 0, :], wgt[:, 1, :], ALU.add))
            op(V.reciprocal(r_b, r_a))
            for j in range(2):
                op(V.tensor_tensor(wgt[:, j, :], wgt[:, j, :], r_b, ALU.mult))
            op(V.memset(r_valid, 1.0))
            op(V.memset(r_valid[:, NTP, :], 0.0))
            op(V.memset(r_valid[0:NS, NTP, :], 1.0))
            op(V.tensor_tensor(r_off, r_h0, r_h1, ALU.add))
            op(V.tensor_tensor(r_mask3, r_off, r_valid, ALU.mult))
            dve.sem_inc(S["r_pos"], 1)
            dve.wait_ge(S["r_m"], 2)
            op(V.memset(r_base[:, 0, :], 0.0))
            tot = bank[:, 1, 0:NT * E].rearrange("p (t e) -> p t e", e=E)
            for t in range(NT):
                op(V.tensor_tensor(r_base[:, t + 1, :], r_base[:, t, :], tot[:, t, :], ALU.add))
            caps = r_cmp[:, 0:E * NCAP].rearrange("p (e j) -> p e j", e=E)
            op(V.tensor_tensor(caps, r_base[:, NT, :].unsqueeze(2).broadcast_to([P, E, NCAP]),
                               row(cap_no, E, NCAP), ALU.is_gt))
            op(V.tensor_reduce(r_nt, caps, AX_X, ALU.add))
            op(V.tensor_tensor_scan(r_end, r_nt, r_nt, 0.0, ALU.add, ALU.bypass))
            ends = r_cmp.rearrange("p (t e) -> p t e", e=E)
            op(V.tensor_tensor(ends, row(r_end, MT, E), tile_no.unsqueeze(2).broadcast_to([P, MT, E]), ALU.is_le))
            op(V.tensor_reduce(r_te, ends, AX_X, ALU.add))
            op(V.tensor_scalar(r_te, r_te, float(E - 1), None, ALU.min))
            op(V.tensor_copy(tile_exp[:, :], r_te))
            even = tile_no.rearrange("p (i s) -> p i s", s=2)[:, :, 0]
            op(V.tensor_scalar(r_te[:, 0:MT // 2], even, r_end[:, E - 1:E], None, ALU.is_lt))
            op(V.tensor_reduce(r_a[:, 0:1], r_te[:, 0:MT // 2], AX_X, ALU.add))
            op(V.tensor_copy(n_pairs[:, :], r_a[:, 0:1]))
            dve.sem_inc(S["tiles_ready"], 1)
            op(V.tensor_tensor(r_t1, r_end, r_nt, ALU.subtract))
            op(V.tensor_scalar(r_t1, r_t1, float(P), None, ALU.mult))
            op(V.tensor_tensor(r_sel, r_base[:, 0:NT, :], row(r_t1, NT, E), ALU.add))
            op(V.tensor_tensor(r_sel, r_sel, bank[:, 0, 0:NT * E].rearrange("p (t e) -> p t e", e=E), ALU.add))
            for j, hot in enumerate((r_h0, r_h1)):
                op(V.tensor_tensor(r_off, r_sel, hot, ALU.mult))
                op(V.tensor_reduce(r_a, r_off, AX_X, ALU.add))
                op(V.tensor_copy(slot_i[:, j, :], r_a))
            dve.sem_inc(S["r_slots"], 1)
            dve.wait_ge(S["tiles_ready"], 1)
            pairs_used = dve.value_load(n_pairs[0:1, 0:1], min_val=1, max_val=MT // 2)

            dve.sem_inc(S["act_done"], 2)
            dve.sem_inc(S["aT_sb"], 1)
            dve.sem_inc(S["y_hi"], 1)
            dve.sem_inc(S["xgT_hi"], 1)
            c.reset()
            with dve.Fori(0, MT // 2) as i, dve.If(i < pairs_used):
                def swish(s):
                    t = 2 * i + s
                    dve.wait_ge(S["g_sig"], t + 3)
                    c.put(V.tensor_tensor(act_t[:, s, :], act_t[:, s, :], bank[:, 2 * s, :], ALU.mult))
                    c.wait()
                    V.tensor_tensor(act_t[:, s, :], act_t[:, s, :], bank[:, 2 * s + 1, :], ALU.mult)\
                        .then_inc(S["act_done"], 1)

                def tail(s):
                    t = 2 * i + s
                    dve.wait_ge(S["aT_ps"], t + 3)
                    dve.wait_ge(S["y_mm"], 2 * t + 2)
                    V.tensor_copy(actT[:, s, :, :], bank[:, 4, :].rearrange("p (k n) -> p k n", k=KF))\
                        .then_inc(S["aT_sb"], 1)

                def out_hi(s):
                    t = 2 * i + s
                    dve.wait_ge(S["y_mm"], 2 * t + 6)
                    dve.wait_ge(y_st[s], 16 * i + 16)
                    V.tensor_copy(y_t[:, s, 512:], bank[:, 7, :]).then_inc(S["y_hi"], 1)

                def turned(s):
                    t = 2 * i + s
                    dve.wait_ge(S["xg_ps"], t + 3)
                    dve.wait_ge(S["gu_mm"], t + 1)
                    V.tensor_copy(xgT[:, s, 4:8, :], bank[:, 5, :].rearrange("p (k n) -> p k n", k=4))\
                        .then_inc(S["xgT_hi"], 1)

                turned(0)
                swish(0)
                turned(1)
                tail(0)
                swish(1)
                tail(1)
                out_hi(0)
                out_hi(1)
                c.reset()
            join(dve, 7)

            for t in range(NT):
                n, kind = (P, 0) if t < NTP else (NS, 1)
                dve.wait_ge(S["y_first"], t + 1)
                yt = ya[0:n, t, :]
                op(V.scalar_tensor_tensor(yt, yb[0:n, t, :], wgt[0:n, 1, t:t + 1], yt, ALU.mult, ALU.add))
                op(V.tensor_tensor(yt, yt, G2[0:n, kind, :], ALU.mult))
                V.tensor_tensor(x1[0:n, t, :], x1[0:n, t, :], yt, ALU.add).then_inc(S["y_sum"], 1)


_INS = ['x_prompt', 'x_sample', 'cache_k', 'cache_v', 'state_conv', 'page_table', 'c_prompt', 'c_sample', 'w_ada',
        'b_ada', 'norm_mix', 'norm_ffn', 'w_in', 'q_norm', 'k_norm', 'sb_bias', 'conv_w', 'conv_b', 'conv_ln_g',
        'conv_ln_b', 'w_out', 'w_router', 'b_router', 'w_gate', 'w_up', 'w_down']


def kernel(**inputs):
    import numpy as _np
    import concourse.bacc as _bacc
    from concourse import mybir as _mybir
    from concourse.bass_utils import run_bass_kernel_spmd as _run

    nc = _bacc.Bacc("TRN2", target_bir_lowering=False, num_devices=1)
    arrays, args = {}, []
    for name in _INS:
        a = _np.ascontiguousarray(inputs[name])
        arrays[f"in_{name}_dram"] = a
        args.append(nc.dram_tensor(f"in_{name}_dram", a.shape, _mybir.dt.from_np(a.dtype), kind="ExternalInput").ap())
    depth, _, _, heads, hd = inputs['cache_k'].shape
    bp, seq, _ = inputs['x_prompt'].shape
    bsm, dseq, _ = inputs['x_sample'].shape
    _, cwid, cch = inputs['conv_w'].shape
    outs = [inputs['x_prompt'].shape, inputs['x_sample'].shape, (depth, bp, seq, heads, hd), (depth, bp, seq, heads, hd),
            (depth, bp, cwid - 1, cch), (depth, bsm, dseq, heads, hd), (depth, bsm, dseq, heads, hd),
            (depth, bsm, cwid - 1, cch)]
    for i, shape in enumerate(outs):
        args.append(nc.dram_tensor(f"out_{i}_dram", shape, _mybir.dt.float32, kind="ExternalOutput").ap())
    decoder_step(nc, *args)
    r = _run(nc, [arrays], core_ids=[0])
    return tuple(r.results[0][f"out_{i}_dram"] for i in range(len(outs)))
```

```python
from contextlib import ExitStack

import concourse.bass as bass
from concourse import mybir

F32 = mybir.dt.float32
BF16 = mybir.dt.bfloat16
I32 = mybir.dt.int32
ALU = mybir.AluOpType
ACT = mybir.ActivationFunctionType
AX_X = mybir.AxisListType.X

P = 128
EPS = 1e-6
NEG = -1.0e30


class Chain:

    def __init__(self, eng, sem):
        self.eng, self.sem, self.n = eng, sem, 0

    def put(self, ins):
        self.n += 1
        ins.then_inc(self.sem, 1)

    def wait(self, back=0):
        if self.n - back > 0:
            self.eng.wait_ge(self.sem, self.n - back)

    def reset(self):
        self.wait()
        self.eng.sem_clear(self.sem)
        self.n = 0


def decoder_step(nc, x_prompt, x_sample, cache_k, cache_v, state_conv, page_table, c_prompt, c_sample,
                 w_ada, b_ada, norm_mix, norm_ffn, w_in, q_norm, k_norm, sb_bias, conv_w, conv_b, conv_ln_g,
                 conv_ln_b, w_out, w_router, b_router, w_gate, w_up, w_down,
                 y_prompt, y_sample, new_k_prompt, new_v_prompt, new_conv_prompt,
                 new_k_sample, new_v_sample, new_conv_sample):
    SEQ, D = x_prompt.shape[1:]
    DB, DS = x_sample.shape[:2]
    NS = DB * DS
    NPOOL, PAGE, H, HD = cache_k.shape[1:]
    NPG = page_table.shape[1]
    PAST = NPG * PAGE
    AW = H * HD
    CW, CC = conv_w.shape[1:]
    TAIL = CW - 1
    E, _, F = w_gate.shape[1:]
    EG = 4
    EPG = E // EG
    KD = D // P
    NTP = SEQ // P
    NT = NTP + 1
    TOK = SEQ + NS
    NPAIR = H // 2
    NCH = CC // P
    NCHUNK = w_in.shape[2] // 512
    NADA = w_ada.shape[2] // D
    MT = (2 * TOK + E * (P - 1)) // P
    MT += MT % 2
    NSLOT = MT * P
    MT_USED = (2 * TOK + 2 * P - 1) // (2 * P) * 2
    KF = F // P
    assert AW == 512 and CC == 512 and D == 1024 and PAGE == P and NS == 32 and F == 512

    mods_d = nc.dram_tensor("mods_d", [1 + DB, NADA * D], F32).ap()
    qT_d = nc.dram_tensor("qT_d", [NPAIR, P, SEQ], F32).ap()
    kT_d = nc.dram_tensor("kT_d", [NPAIR, P, SEQ], F32).ap()
    h2_d = nc.dram_tensor("h2_d", [TOK, D], F32).ap()
    y_d = nc.dram_tensor("y_d", [NSLOT, D], F32).ap()

    xp, xs = x_prompt[0], x_sample.rearrange("a b d -> (a b) d")
    yp, ys = y_prompt[0], y_sample.rearrange("a b d -> (a b) d")
    kp_out = new_k_prompt[0, 0].rearrange("n h d -> n (h d)")
    vp_out = new_v_prompt[0, 0].rearrange("n h d -> n (h d)")
    ks_out = new_k_sample[0].rearrange("b n h d -> (b n) (h d)")
    vs_out = new_v_sample[0].rearrange("b n h d -> (b n) (h d)")
    ck = cache_k[0].rearrange("n p h d -> n p (h d)")
    cv = cache_v[0].rearrange("n p h d -> n p (h d)")

    def rows_of(vec, parts, reps=1, width=None, offset=0):
        width = width or vec.shape[-1]
        return bass.AP(vec.tensor, vec.offset + offset, [[0, parts], [0, reps], [1, width]])

    ctx = ExitStack()
    with ctx:
        def sb(name, shape, dt=F32):
            return ctx.enter_context(nc.sbuf_tensor(name, shape, dt))

        def sem(name):
            return ctx.enter_context(nc.semaphore(name))

        big = sb("big", [P, 24576])
        mid = sb("mid", [P, 8192])
        low = sb("low", [P, 9400])
        cvT = sb("cvT", [P, NCH, TOK])
        xt = sb("xt", [P, 2, D])
        G2 = sb("G2", [P, 2, D])
        identf = sb("identf", [P, P])
        identb = sb("identb", [P, P], BF16)
        causal = sb("causal", [P, P], BF16)
        before = sb("before", [P, P], BF16)
        onesb = sb("onesb", [P, P], BF16)
        q_of_row = sb("q_of_row", [DS, H, DS], BF16)
        mean_of = sb("mean_of", [P, P])
        mhalf = sb("mhalf", [P, 16])
        cT = sb("cT", [P, KD, 16])
        cw = sb("cw", [P, NCH, 36])
        bb = sb("bb", [P, H])
        nbb = sb("nbb", [P, H])
        bs = sb("bs", [NS, 1])
        nbs = sb("nbs", [NS, 1])
        pt = sb("pt", [1, DB * NPG], I32)
        st = sb("st", [P, 64])
        qTs = sb("qTs", [P, NPAIR, NS])
        kTs = sb("kTs", [P, NPAIR, NS])
        wr = sb("wr", [P, KD, E])
        br = sb("br", [P, E])
        logits = sb("logits", [P, NT, E])
        slot_tok = sb("slot_tok", [P, MT + 1], I32)
        tile_of = sb("tile_of", [P, 2 * NT], I32)
        tok_part_i = sb("tok_part_i", [P, 2, NT], I32)
        slot_i = sb("slot_i", [P, 2, NT], I32)
        wgt = sb("wgt", [P, 2, NT])
        tile_exp = sb("tile_exp", [P, MT], I32)
        n_pairs = sb("n_pairs", [P, 1], I32)
        NCAP = (TOK + P - 1) // P
        ramp_i = sb("ramp_i", [P, MT + EG + E + NCAP + P], I32)
        ramp = sb("ramp", [P, MT + EG + E + NCAP + P])
        tile_no, g_rank = ramp[:, 0:MT], ramp[:, MT:MT + EG]
        e_rank, cap_no = ramp[:, MT + EG:MT + EG + E], ramp[:, MT + EG + E:MT + EG + E + NCAP]
        row_no = ramp[:, MT + EG + E + NCAP:]
        col_tok = sb("col_tok", [P, 2], I32)
        bank = ctx.enter_context(nc.psum_tensor("bank", [P, 8, 512], F32))
        flat = bank[:, :, :].rearrange("p b n -> p (b n)")

        ada = mid[:, :].rearrange("p (s k n) -> p s k n", s=4, k=4)
        A0 = 20480
        w_in_sb = big[:, 0:A0].rearrange("p (k n) -> p k n", k=KD)
        c9 = big[0:1 + DB, A0:A0 + D]
        csig = big[0:1 + DB, A0 + D:A0 + 2 * D]
        mrow = G2[0:1 + DB, 1, :]
        brow = big[0:1 + DB, A0 + 3 * D:A0 + 4 * D]
        hrow = big[:, A0:A0 + 2 * D].rearrange("p (s n) -> p s n", s=2)
        hT = big[:, A0 + 2 * D:A0 + 4 * D].rearrange("p (s k n) -> p s k n", s=2, k=KD)
        qk_t = mid[:, 0:2048].rearrange("p (s n) -> p s n", s=2)
        v_t = mid[:, 2048:3072].rearrange("p (s n) -> p s n", s=2)
        glu_t = mid[:, 3072:4096].rearrange("p (s n) -> p s n", s=2)
        sg_t = mid[:, 4096:5120].rearrange("p (s n) -> p s n", s=2)
        sq_t = mid[:, 5120:6144]
        qT_t = mid[:, 6144:6656]
        kT_t = mid[:, 6656:7168]
        qkw = mid[:, 7168:8192]
        GX = TAIL + SEQ
        glu_x = low[:, 0:NCH * GX].rearrange("p (c n) -> p c n", c=NCH)
        SX = TAIL + DS
        G0 = NCH * GX
        glu_s = low[:, G0:G0 + NCH * DB * SX].rearrange("p (c b n) -> p c b n", c=NCH, b=DB)
        B0 = G0 + NCH * DB * SX
        AB = low[:, B0:B0 + 4 * D].rearrange("p (s w n) -> p s w n", s=2, w=2)
        ln_a = big[:, 12288:14336].rearrange("p (c n) -> p c n", c=NCH)
        ln_b = big[:, 14336:16384].rearrange("p (c n) -> p c n", c=NCH)
        ln_v = big[:, 16384:16896]
        ln_r = big[:, 16896:17408]
        stage = big[:, 0:6144].rearrange("p (s w n) -> p s w n", s=2, w=3)
        sig = big[:, 6144:8192].rearrange("p (s n) -> p s n", s=2)
        keep = big[:, 8192:10240].rearrange("p (s n) -> p s n", s=2)
        prod = big[:, 10240:12292].rearrange("p (s n) -> p s n", s=2)
        aT = big[:, 12292:14340].rearrange("p (s n) -> p s n", s=2)
        O0 = 24576 - NPAIR * TOK
        oT = big[:, O0:].rearrange("p (c n) -> p c n", c=NPAIR)
        KN = PAST + DS
        sig_s = big[0:NS, 16388:16388 + KN]
        keep_s = big[0:NS, 17416:17416 + KN]
        prod_s = big[0:NS, 18444:18444 + KN + 1]
        aT_s = big[:, 19474:19474 + (NPG + 1) * NS].rearrange("p (g n) -> p g n", n=NS)
        S0 = 19474 + (NPG + 1) * NS
        o_all = big[0:NS, S0:S0 + AW]
        v_new = xt[0:DS, 1, 0:AW]
        q_bd = xt[:, 0, :].rearrange("p (b c n) -> p b c n", b=DB, c=NPAIR)
        q_stage = sb("q_stage", [P, NPAIR, NS])
        kT = mid[:, 0:NPAIR * KN].rearrange("p (c n) -> p c n", c=NPAIR)
        k_pg = [v[:, n0 + g * AW:n0 + (g + 1) * AW]
                for v, n0 in ((big, 14340), (mid, NPAIR * KN)) for g in range(NPG // 2)]
        v_pg = low[:, B0:B0 + NPG * AW].rearrange("p (g n) -> p g n", g=NPG)
        w_out_sb = mid[:, :].rearrange("p (k n) -> p k n", k=KD)
        mod2 = big[:, 0:6144].rearrange("p (w s n) -> p w s n", w=3, s=2)
        h2 = big[:, 6144:8192].rearrange("p (s n) -> p s n", s=2)
        h2T = big[:, 8192:10240].rearrange("p (s k n) -> p s k n", s=2, k=KD)
        sqx = big[:, 10240:11264]
        gffn = big[:, 11264:12288]
        lgT = big[0:E, 17408:17408 + TOK]
        x1 = low[:, 0:NT * D].rearrange("p (t n) -> p t n", t=NT)
        R0 = [4096]

        def small(*shape):
            n = 1
            for k in shape:
                n *= k
            v = mid[:, R0[0]:R0[0] + n]
            R0[0] += n
            if len(shape) == 2:
                v = v.rearrange("p (a b) -> p a b", a=shape[0])
            if len(shape) == 3:
                v = v.rearrange("p (a b c) -> p a b c", a=shape[0], b=shape[1])
            return v

        r_a, r_b = small(NT), small(NT)
        r_z, r_e, r_p, r_sel, r_off, r_h0, r_h1, r_valid = (small(NT, E) for _ in range(8))
        r_hi, r_lo = small(NT * EG * 2), small(NT * EG * 2)
        r_gs, r_g1 = small(NT * EG), small(NT * EG)
        r_cmp = small(MT * E)
        r_base = small(NT + 1, E)
        r_nt, r_end, r_t1 = small(E), small(E), small(E)
        r_te = small(MT)
        r_part, r_slot, r_row, r_tile = (small(2 * NT) for _ in range(4))
        r_id, r_tok = small(2 * MT), small(MT)
        assert R0[0] <= 8192
        r_maskb = sb("r_maskb", [P, NT * E], BF16)[:, :]
        r_mask3 = r_maskb.rearrange("p (t e) -> p t e", e=E)
        at_row = mid[:, 0:NT * P].bitcast(BF16).rearrange("p (a n) -> p a n", n=P)
        at_tile = mid[:, NT * P:NT * P + NT * MT].bitcast(BF16).rearrange("p (a n) -> p a n", n=MT)
        tile_id = mid[:, NT * (P + MT):NT * (P + 3 * MT)].bitcast(BF16).rearrange("p (a w n) -> p a w n", w=2, n=MT)
        assert NT * (P + 3 * MT) <= 4096
        wts = big[:, :].rearrange("p (s n) -> p s n", s=2)
        wg_sb = wts[:, :, 0:4096].rearrange("p s (k n) -> p s k n", k=KD)
        wu_sb = wts[:, :, 4096:8192].rearrange("p s (k n) -> p s k n", k=KD)
        wd_sb = wts[:, :, 8192:12288].rearrange("p s (k n) -> p s k n", k=KF)
        xg = mid[:, 0:2048].rearrange("p (s n) -> p s n", s=2)
        xgT = mid[:, 2048:4096].rearrange("p (s k n) -> p s k n", s=2, k=KD)
        act_t = mid[:, 4096:5120].rearrange("p (s n) -> p s n", s=2)
        actT = mid[:, 5120:6144].rearrange("p (s k n) -> p s k n", s=2, k=KF)
        y_t = mid[:, 6144:8192].rearrange("p (s n) -> p s n", s=2)
        ya = big[:, 0:NT * D].rearrange("p (t n) -> p t n", t=NT)
        yb = big[:, NT * D:2 * NT * D].rearrange("p (t n) -> p t n", t=NT)

        phase = sem("phase")
        settled = sem("settled")
        names = ("const_in pool_const c_sig c_silu cT_ps cT_sb st_ps st_sb brow_in ada_used rows_done "
                 "rows_stored mod1_in "
                 "x_sq x_var x_rstd h_ready hT_ps hT_sb mm_chunk sg_done glu_done qk_sq qk_var qk_rstd qk_scaled "
                 "qk_done v_done post_ps glu_sb q_sb k_sb qkT_st conv_st "
                 "ln_mean ln_cent ln_sq ln_var ln_dv ln_std ln_norm ln_sig ln_done "
                 "qk_mm keep_done sig_done scan_done a_done at_ps at_sb pv_mm o_sb w_attn_in w_conv_in zero_y "
                 "kt_even kt_odd kt_act kt_dve q_staged qbd_done s_mm s_keep s_sig s_sig_new s_scan s_a s_at s_at_sb s_pv s_o_all s_o_ps s_o "
                 "mod2_in mix_mm x1_tmp x1_done x2_sq x2_var x2_rstd h2_done h2_ps h2T_sb lg_mm lg_sb "
                 "r_ready r_m tok_ready col_ready exp_ready tiles_ready "
                 "xg_ps xgT_sb xgT_hi gu_mm g_sig act_done aT_ps aT_sb y_mm y_lo y_hi y_first y_gated y_sum y_sum_pool out_st "
                 "v_in dve_c pool_c").split()
        S = {n: sem(n) for n in names}
        ada_in = [sem(f"ada_in{i}") for i in range(4)]
        x_in = [sem(f"x_in{i}") for i in range(2)]
        kv_st = [sem(f"kv_st{i}") for i in range(2)]
        stage_in = [sem(f"stage_in{i}") for i in range(2)]
        k_in = [sem(f"k_in{i}") for i in range(NPG)]
        w_in_in = [sem(f"w_in_in{i}") for i in range(NCHUNK)]
        h2_stored = [sem(f"h2_stored{i}") for i in range(2)]
        wg_in = [sem(f"wg_in{i}") for i in range(2)]
        wu_in = [sem(f"wu_in{i}") for i in range(2)]
        wd_in = [sem(f"wd_in{i}") for i in range(2)]
        xg_in = [sem(f"xg_in{i}") for i in range(2)]
        y_st = [sem(f"y_st{i}") for i in range(2)]
        ya_in = [sem(f"ya_in{i}") for i in range(NT)]

        CHUNKS = (3, 4, 0, 1, 2)
        POOL_ADDS = (3, 4, 5, 6)
        ENGINES = 5
        N_CONST = 13
        LN_AT = {1: 0, 2: 4}
        LN_COLS = [(c0, min(512, TOK - c0)) for c0 in range(0, TOK, 512)]

        def join(eng, n):
            eng.drain().then_inc(phase, 1)
            eng.wait_ge(phase, ENGINES * n)

        def settle(eng):
            eng.sem_inc(settled, 1)

        block = ctx.enter_context(nc.Block())
        UNITS = 2 * NTP
        ROUNDS = NPAIR // 2
        RU = 2 * UNITS
        RSEQ = DB // ROUNDS
        SU = RU // RSEQ
        S_AT = SU - 2
        assert SU == NTP == NPG and NTP == 8

        def odd_page(u):
            return 2 * (u % SU) + 1 if u % SU < SU // 2 else None

        def even_page(u):
            return 2 * (u % SU) - 2 if 1 <= u % SU <= SU // 2 else None

        def place(u):
            return u + (u + SU - S_AT) // SU

        def place_s(r):
            return place(r * SU + S_AT) - 1

        @block.sync
        def _(sp):
            n_const = [0]

            def const(dst, src):
                n_const[0] += 16
                sp.dma_start(dst, src).then_inc(S["const_in"], 16)

            const(c9[0:1, :], c_prompt)
            const(c9[1:1 + DB, :], c_sample)
            const(xt[0:CW, 0, 0:CC], conv_w[0])
            const(xt[CW:CW + 1, 0, 0:CC], conv_b)
            const(xt[CW + 1:CW + 2, 0, 0:CC], conv_ln_g)
            const(xt[CW + 2:CW + 3, 0, 0:CC], conv_ln_b)
            half_b = DB // 2
            for j in range(2):
                const(xt[0:half_b * TAIL, 1, j * CC:(j + 1) * CC],
                      state_conv[0, j * half_b:(j + 1) * half_b].rearrange("b n c -> (b n) c"))
            const(bb[:, :], bass.AP(sb_bias.tensor, 0, [[0, P], [1, H]]))
            const(bs[:, :], bass.AP(sb_bias.tensor, 0, [[1, H], [0, DS], [1, 1]]))
            const(pt[:, :], page_table.rearrange("b g -> (b g)").rearrange("(a n) -> a n", a=1))
            const(wr[:, :, :], w_router.rearrange("(k p) e -> p k e", p=P))
            const(br[:, :], bass.AP(b_router.tensor, 0, [[0, P], [1, E]]))
            assert n_const[0] == 16 * N_CONST
            with sp.Fori(0, NADA) as i:
                for s in range(4):
                    c, kh = s // 2, s % 2
                    sp.wait_ge(S["ada_used"], 4 * i + s + 1)
                    sp.dma_start(ada[:, s, :, :],
                                 w_ada[0, kh * 512:(kh + 1) * 512, bass.ds(i * D + c * 512, 512)]
                                 .rearrange("(k p) n -> p k n", p=P)).then_inc(ada_in[s], 16)
                sp.wait_ge(S["rows_done"], 2 * i + 2)
                sp.dma_start(brow, bass.AP(b_ada.tensor, 0, [[0, 1 + DB], [1, NADA * D]])[:, bass.ds(i * D, D)])\
                    .then_inc(S["brow_in"], 16)
            sp.wait_ge(S["rows_stored"], 16 * (1 + 2))
            def mod_rows(dst, w, kind):
                if kind == 0:
                    src = bass.AP(mods_d.tensor, w * D, [[0, P], [1, D]])
                else:
                    src = bass.AP(mods_d.tensor, NADA * D + w * D, [[NADA * D, DB], [0, DS], [1, D]])
                return dst, src
            for kind, parts in ((0, P), (1, NS)):
                for w in range(2):
                    sp.dma_start(*mod_rows(AB[0:parts, kind, w, :], 1 - w, kind)).then_inc(S["mod1_in"], 16)
            sp.dma_start(hrow[:, 0, :], bass.AP(norm_mix.tensor, 0, [[0, P], [1, D]])).then_inc(S["mod1_in"], 16)
            sp.wait_ge(S["st_ps"], 1)
            for t in range(2):
                sp.dma_start(xt[:, t, :], xp[t * P:(t + 1) * P, :]).then_inc(x_in[t], 16)
            for cc in CHUNKS:
                sp.dma_start(w_in_sb[:, :, cc * 512:(cc + 1) * 512],
                             w_in[0, :, cc * 512:(cc + 1) * 512].rearrange("(k p) n -> p k n", p=P))\
                    .then_inc(w_in_in[cc], 16)
            join(sp, 1)
            sp.dma_start(new_conv_sample[0, :, 0:TAIL - DS, :], state_conv[0, :, DS:TAIL, :]).then_inc(S["conv_st"], 16)
            sp.dma_start(qkw[:, 0:AW].rearrange("p (h d) -> p h d", h=H), rows_of(q_norm, P, H)).then_inc(S["mod1_in"], 16)
            sp.dma_start(qkw[:, AW:].rearrange("p (h d) -> p h d", h=H), rows_of(k_norm, P, H)).then_inc(S["mod1_in"], 16)

            def load_x(t):
                s = t % 2
                sp.wait_ge(S["h_ready"], t - 1)
                if t < NTP:
                    sp.dma_start(xt[:, s, :], xp[t * P:(t + 1) * P, :]).then_inc(x_in[s], 16)
                elif t == NTP:
                    sp.dma_start(xt[0:NS, s, :], xs).then_inc(x_in[s], 16)

            def stage_pair(pair, s):
                sp.dma_start(stage[:, s, 0, :], qT_d[bass.ds(pair, 1), :, :].rearrange("a p n -> (a p) n"))\
                    .then_inc(stage_in[s], 16)
                sp.dma_start(stage[:, s, 1, :], kT_d[bass.ds(pair, 1), :, :].rearrange("a p n -> (a p) n"))\
                    .then_inc(stage_in[s], 16)
                sp.dma_start(stage[:, s, 2, :].rearrange("p (b n) -> p b n", b=NTP),
                             vp_out[:, bass.ds(pair * P, P)].rearrange("(b p) n -> p b n", p=P))\
                    .then_inc(stage_in[s], 16)

            def store_tile(t):
                s = t % 2
                n = P if t < NTP else NS
                ko, vo = (kp_out[t * P:(t + 1) * P, :], vp_out[t * P:(t + 1) * P, :]) if t < NTP else (ks_out, vs_out)
                sp.wait_ge(S["qk_done"], t + 1)
                sp.dma_start(ko, qk_t[0:n, s, AW:]).then_inc(kv_st[s], 16)
                sp.wait_ge(S["v_done"], t + 1)
                sp.dma_start(vo, v_t[0:n, s, :]).then_inc(kv_st[s], 16)
                if t == NTP - 1:
                    sp.dma_start(new_conv_prompt[0, 0], glu_t[P - TAIL:P, s, :]).then_inc(S["conv_st"], 16)
                if t == NTP:
                    sp.dma_start(bass.AP(new_conv_sample.tensor, (TAIL - DS) * CC, [[TAIL * CC, DB], [CC, DS], [1, CC]]),
                                 glu_t[0:NS, s, :]).then_inc(S["conv_st"], 16)
                if t < NTP:
                    sp.wait_ge(S["q_sb"], t + 1)
                    sp.dma_start(qT_d.rearrange("c p n -> p c n")[:, :, t * P:(t + 1) * P],
                                 qT_t.rearrange("p (c n) -> p c n", c=NPAIR)).then_inc(S["qkT_st"], 16)
                    sp.wait_ge(S["k_sb"], t + 1)
                    sp.dma_start(kT_d.rearrange("c p n -> p c n")[:, :, t * P:(t + 1) * P],
                                 kT_t.rearrange("p (c n) -> p c n", c=NPAIR)).then_inc(S["qkT_st"], 16)

            for t in range(NT):
                load_x(t + 2)
                if t >= 1:
                    store_tile(t - 1)
            sp.wait_ge(S["mm_chunk"], NCHUNK * NT)
            sp.wait_ge(kv_st[(NTP - 1) % 2], 32 * (NTP // 2))
            sp.wait_ge(kv_st[NTP % 2], 32 * (NTP // 2))
            sp.wait_ge(S["qkT_st"], 32 * NTP)
            stage_pair(0, 0)
            store_tile(NT - 1)
            sp.wait_ge(kv_st[0], 32 * 5)
            sp.wait_ge(kv_st[1], 32 * 4)
            sp.wait_ge(S["qkT_st"], 32 * NTP)
            sp.wait_ge(S["conv_st"], 16 * 3)
            sp.wait_ge(S["rows_stored"], 16 * (NADA + 1))
            join(sp, 2)

            with sp.Fori(0, ROUNDS) as i:
                for r in range(RSEQ):
                    b = RSEQ * i + r
                    pages = []
                    for g in range(NPG):
                        pages.append(sp.value_load(pt[0:1, bass.ds(b * NPG + g, 1)], min_val=0, max_val=NPOOL - 1))
                        sp.wait_ge(S[("kt_even", "kt_odd")[g % 2]], 4 * b + g // 2 + 1)
                        sp.dma_start(k_pg[g], ck[bass.ds(pages[g], 1), :, :]
                                     .rearrange("a p n -> (a p) n")).then_inc(k_in[g], 16)
                    if r == 0:
                        sp.wait_ge(S["pv_mm"], i * RU + UNITS + 2)
                        stage_pair(2 * i + 1, 1)
                    sp.wait_ge(S["s_pv"], b + 1)
                    for g in range(NPG):
                        sp.dma_start(v_pg[:, g, :], cv[bass.ds(pages[g], 1), :, :].rearrange("a p n -> (a p) n"))\
                            .then_inc(S["v_in"], 16)
                    sp.dma_start(v_new, vs_out[bass.ds(b * DS, DS), :]).then_inc(S["v_in"], 16)
                with sp.If(i < ROUNDS - 1):
                    sp.wait_ge(S["pv_mm"], (i + 1) * RU + 2)
                    stage_pair(nc.s_assert_within(2 * i + 2, 0, NPAIR - 1, skip_runtime_bounds_check_because=
                                                  "i is below ROUNDS - 1 here"), 0)
            join(sp, 3)

            for k in range(KD):
                sp.dma_start(w_out_sb[:, k, :], w_out[0, k * P:(k + 1) * P, :])\
                    .then_inc(S[("w_attn_in", "w_conv_in")[k // NPAIR]], 16)
            for w in range(3):
                for kind, parts in ((0, P), (1, NS)):
                    sp.dma_start(*mod_rows(mod2[0:parts, w, kind, :], (2, 4, 3)[w], kind)).then_inc(S["mod2_in"], 16)
            for kind, parts in ((0, P), (1, NS)):
                sp.dma_start(*mod_rows(G2[0:parts, kind, :], 5, kind)).then_inc(S["mod2_in"], 16)
            sp.dma_start(gffn, bass.AP(norm_ffn.tensor, 0, [[0, P], [1, D]])).then_inc(S["mod2_in"], 16)

            def load_x2(t):
                s = t % 2
                if t >= 2:
                    sp.wait_ge(S["x1_done"], t - 1)
                n, src = (P, xp[t * P:(t + 1) * P, :]) if t < NTP else (NS, xs)
                sp.dma_start(xt[0:n, s, :], src).then_inc(x_in[s], 16)

            def store_h2(t):
                n = P if t < NTP else NS
                sp.wait_ge(S["h2_done"], t + 1)
                sp.dma_start(h2_d[t * P:t * P + n, :], h2[0:n, t % 2, :]).then_inc(h2_stored[t % 2], 16)

            load_x2(0)
            load_x2(1)
            for t in range(NT):
                if t + 2 < NT:
                    load_x2(t + 2)
                store_h2(t)
            sp.wait_ge(h2_stored[0], 16 * 5)
            sp.wait_ge(h2_stored[1], 16 * 4)
            join(sp, 4)
            sp.wait_ge(S["tiles_ready"], 1)
            pairs_used = sp.value_load(n_pairs[0:1, 0:1], min_val=1, max_val=MT // 2)

            with sp.Fori(0, MT // 2) as i, sp.If(i < pairs_used):
                experts = [sp.value_load(tile_exp[0:1, bass.ds(2 * i + s, 1)], min_val=0, max_val=E - 1)
                           for s in range(2)]
                for s in range(2):
                    e = bass.ds(experts[s], 1)
                    sp.wait_ge(S["gu_mm"], 2 * i + s + 1)
                    sp.dma_start(wg_sb[:, s, :, :], w_gate[0, e, :, :].rearrange("a (k p) n -> p (a k) n", p=P))\
                        .then_inc(wg_in[s], 16)
                    sp.wait_ge(S["col_ready"], 2 * i + 2)
                    sp.dma_start(wu_sb[:, s, :, :], w_up[0, e, :, :].rearrange("a (k p) n -> p (a k) n", p=P))\
                        .then_inc(wu_in[s], 16)
                for s in range(2):
                    e = bass.ds(experts[s], 1)
                    sp.wait_ge(S["y_mm"], 4 * i + 2 * s + 2)
                    sp.dma_start(wd_sb[:, s, :, :], w_down[0, e, :, :].rearrange("a (k p) n -> p (a k) n", p=P))\
                        .then_inc(wd_in[s], 16)
            join(sp, 5)

            for t in range(NT):
                n, dst = (P, yp[t * P:(t + 1) * P, :]) if t < NTP else (NS, ys)
                if t in POOL_ADDS:
                    sp.wait_ge(S["y_sum_pool"], POOL_ADDS.index(t) + 1)
                else:
                    sp.wait_ge(S["y_sum"], 1 + sum(k not in POOL_ADDS for k in range(t)))
                sp.dma_start(dst, x1[0:n, t, :]).then_inc(S["out_st"], 16)
            sp.wait_ge(S["out_st"], 16 * NT)

        @block.gpsimd
        def _(pool):
            c = Chain(pool, S["pool_c"])
            c.put(pool.memset(identf[:, :], 0.0))
            c.put(pool.memset(identb[:, :], 0.0))
            c.put(pool.memset(causal[:, :], 0.0))
            c.put(pool.memset(before[:, :], 1.0))
            c.put(pool.memset(q_of_row[:, :, :], 0.0))
            pool.memset(onesb[:, :], 1.0)
            pool.memset(mean_of[:, :], 1.0 / CC)
            pool.memset(mhalf[:, :], -0.5)
            pool.memset(G2[:, 0, :], 0.0)
            pool.memset(glu_x[:, :, 0:TAIL], 0.0)
            c.wait()
            for m in (identf, identb):
                pool.affine_select(out=m[:, :], in_=m[:, :], compare_op=ALU.not_equal, fill=1.0, base=0,
                                   pattern=[[-1, P]], channel_multiplier=1)
            pool.affine_select(out=causal[:, :], in_=causal[:, :], compare_op=ALU.is_gt, fill=NEG, base=0,
                               pattern=[[-1, P]], channel_multiplier=1)
            pool.affine_select(out=before[:, :], in_=before[:, :], compare_op=ALU.is_gt, fill=0.0, base=0,
                               pattern=[[1, P]], channel_multiplier=-1)
            pool.affine_select(out=q_of_row[:, :, :], in_=q_of_row[:, :, :], compare_op=ALU.not_equal, fill=1.0,
                               base=0, pattern=[[0, H], [-1, DS]], channel_multiplier=1)
            for v, base, step in ((ramp_i[:, 0:MT], 0, 1), (ramp_i[:, MT:MT + EG], EG, -1),
                                  (ramp_i[:, MT + EG:MT + EG + E], E, -1),
                                  (ramp_i[:, MT + EG + E:MT + EG + E + NCAP], 0, P),
                                  (ramp_i[:, MT + EG + E + NCAP:], 0, 1)):
                pool.iota(v, pattern=[[step, v.shape[1]]], base=base, channel_multiplier=0)
            pool.iota(tok_part_i[:, 0, :], pattern=[[1, NT]], base=0, channel_multiplier=0)
            pool.iota(tok_part_i[:, 1, :], pattern=[[0, NT]], base=0, channel_multiplier=1)\
                .then_inc(S["pool_const"], 1)
            join(pool, 1)

            def rstd_x(t):
                pool.wait_ge(S["x_var"], t + 1)
                pool.tensor_tensor(st[:, 2 + t % 2:3 + t % 2], st[:, t % 2:t % 2 + 1], mhalf[:, 0:1], ALU.pow)\
                    .then_inc(S["x_rstd"], 1)

            rstd_x(0)
            rstd_x(1)
            for t in range(NT):
                pool.wait_ge(S["qk_var"], t + 1)
                pool.tensor_tensor(st[:, 32:48], st[:, 16:32], mhalf[:, :], ALU.pow).then_inc(S["qk_rstd"], 1)
                pool.wait_ge(S["qk_scaled"], t + 1)
                if t == 0:
                    pool.wait_ge(S["mod1_in"], 16 * 7)
                pool.tensor_tensor(qk_t[:, t % 2, :], qk_t[:, t % 2, :], qkw, ALU.mult).then_inc(S["qk_done"], 1)
                if t + 2 < NT:
                    rstd_x(t + 2)
            join(pool, 2)
            pool.wait_ge(S["s_pv"], 2)
            for t in range(MT_USED, MT):
                pool.dma_start(y_d[t * P:(t + 1) * P, :], G2[:, 0, :]).then_inc(S["zero_y"], 16)
            pool.wait_ge(S["zero_y"], 16 * (MT - MT_USED))
            join(pool, 3)
            for t in range(NT):
                pool.wait_ge(S["x1_tmp"], t + 1)
                pool.wait_ge(x_in[t % 2], 16 * ((NT + 1 - t % 2) // 2 + t // 2 + 1))
                n = P if t < NTP else NS
                pool.tensor_tensor(x1[0:n, t, :], x1[0:n, t, :], xt[0:n, t % 2, :], ALU.add)\
                    .then_inc(S["x1_done"], 1)
                pool.wait_ge(S["x2_var"], t + 1)
                pool.tensor_tensor(st[:, 2:3], st[:, 0:1], mhalf[:, 0:1], ALU.pow).then_inc(S["x2_rstd"], 1)
            join(pool, 4)
            pool.wait_ge(S["tiles_ready"], 1)
            pairs_used = pool.value_load(n_pairs[0:1, 0:1], min_val=1, max_val=MT // 2)
            pool.wait_ge(S["tok_ready"], 1)

            def gather_x(t, s):
                pool.wait_ge(S["xg_ps"], t + 1)
                settle(pool)
                pool.tensor_copy(col_tok[:, s:s + 1], slot_tok[:, bass.ds(t, 1)]).then_inc(S["col_ready"], 1)
                pool.wait_ge(S["col_ready"], t + 1)
                settle(pool)
                pool.indirect_dma_start(
                    out=xg[:, s, :], out_offset=None, in_=h2_d,
                    in_offset=bass.IndirectOffsetOnAxis(ap=col_tok[:, s:s + 1], axis=0)).then_inc(xg_in[s], 16)

            gather_x(0, 0)
            with pool.Fori(0, MT // 2) as i, pool.If(i < pairs_used):
                gather_x(2 * i + 1, 1)
                gather_x(2 * i + 2, 0)
            join(pool, 5)
            for t in range(NT):
                n = P if t < NTP else NS
                for j, buf in enumerate((ya, yb)):
                    pool.indirect_dma_start(
                        out=buf[0:n, t, :], out_offset=None, in_=y_d,
                        in_offset=bass.IndirectOffsetOnAxis(ap=slot_i[0:n, j, t:t + 1], axis=0))\
                        .then_inc(ya_in[t], 16)
            for k, t in enumerate(POOL_ADDS):
                pool.wait_ge(S["y_gated"], k + 1)
                pool.tensor_tensor(x1[:, t, :], x1[:, t, :], ya[:, t, :], ALU.add).then_inc(S["y_sum_pool"], 1)

        @block.scalar
        def _(act):
            act.sem_inc(S["rows_stored"], 16)
            act.wait_ge(S["const_in"], 16 * N_CONST)
            nc.scalar.activation(csig, c9, ACT.Sigmoid).then_inc(S["c_sig"], 1)
            act.wait_ge(S["cT_ps"], 1)
            nc.scalar.activation(cT[:, :, 0:1 + DB],
                                 bank[:, 0, 0:KD * 16].rearrange("p (k n) -> p k n", k=KD)[:, :, 0:1 + DB],
                                 ACT.Copy).then_inc(S["cT_sb"], 1)
            act.wait_ge(S["st_ps"], 1)
            nc.scalar.activation(cw[:, :, 0:CW + 3],
                                 bank[:, 1, 0:NCH * 64].rearrange("p (k n) -> p k n", k=NCH)[:, :, 0:CW + 3],
                                 ACT.Copy).then_inc(S["st_sb"], 1)
            for j in range(2):
                for ch in range(NCH):
                    nc.scalar.activation(
                        glu_s[:, ch, 4 * j:4 * j + 4, 0:TAIL],
                        bank[:, 4 + j, ch * 120:(ch + 1) * 120].rearrange("p (b n) -> p b n", b=4),
                        ACT.Copy).then_inc(S["st_sb"], 1)
            nc.scalar.activation(nbb[:, :], bb[:, :], ACT.Copy, scale=-1.0)
            nc.scalar.activation(nbs[:, :], bs[:, :], ACT.Copy, scale=-1.0)
            with act.Fori(0, NADA) as i:
                act.wait_ge(S["rows_done"], 2 * i + 4)
                act.dma_start(mods_d[:, bass.ds(i * D, D)], mrow).then_inc(S["rows_stored"], 16)
            join(act, 1)

            def square_x(t):
                act.wait_ge(x_in[t % 2], 16 * (t // 2 + 1))
                if t >= 2:
                    act.wait_ge(S["hT_ps"], t - 1)
                    act.wait_ge(S["x_var"], t - 1)
                nc.scalar.activation(hrow[:, t % 2, :], xt[:, t % 2, :], ACT.Square,
                                     accum_out=st[:, 4 + t % 2:5 + t % 2]).then_inc(S["x_sq"], 1)

            def evac_hT(t):
                act.wait_ge(S["hT_ps"], t + 1)
                if t >= 2:
                    act.wait_ge(S["mm_chunk"], NCHUNK * (t - 1))
                for j in range(2):
                    nc.scalar.activation(hT[:, t % 2, 4 * j:4 * j + 4, :],
                                         bank[:, 5 + j, :].rearrange("p (k n) -> p k n", k=4),
                                         ACT.Copy).then_inc(S["hT_sb"], 1)

            def evac_post(t):
                if t < NTP:
                    act.wait_ge(S["post_ps"], 3 * t + 1)
                    nc.scalar.activation(glu_x[:, :, TAIL + t * P:TAIL + (t + 1) * P],
                                         bank[:, 7, :].rearrange("p (k n) -> p k n", k=NCH), ACT.Copy)\
                        .then_inc(S["glu_sb"], 1)
                    for j, (dst, done) in enumerate(((qT_t, "q_sb"), (kT_t, "k_sb"))):
                        act.wait_ge(S["post_ps"], 3 * t + 2 + j)
                        if t >= 1:
                            act.wait_ge(S["qkT_st"], 32 * t)
                        nc.scalar.activation(dst, bank[:, 5 + j, :], ACT.Copy).then_inc(S[done], 1)
                else:
                    act.wait_ge(S["post_ps"], 3 * t + 3)
                    for ch in range(NCH):
                        nc.scalar.activation(glu_s[:, ch, :, TAIL:],
                                             bank[:, 7, ch * P:ch * P + NS].rearrange("p (b n) -> p b n", b=DB),
                                             ACT.Copy).then_inc(S["glu_sb"], 1)
                    for j, (dst, done) in enumerate(((qTs, "q_sb"), (kTs, "k_sb"))):
                        nc.scalar.activation(dst[:, :, :],
                                             bank[:, 5 + j, :].rearrange("p (k n) -> p k n", k=NPAIR)[:, :, 0:NS],
                                             ACT.Copy).then_inc(S[done], 1)

            square_x(0)
            square_x(1)
            evac_hT(0)
            for t in range(NT):
                s = t % 2
                act.wait_ge(S["mm_chunk"], NCHUNK * t + 2)
                if t >= 2:
                    act.wait_ge(S["glu_done"], t - 1)
                nc.scalar.activation(sg_t[:, s, :], bank[:, 4, :], ACT.Sigmoid).then_inc(S["sg_done"], 1)
                if t >= 1:
                    evac_post(t - 1)
                if t + 1 < NT:
                    evac_hT(t + 1)
                if t + 2 < NT:
                    square_x(t + 2)
                act.wait_ge(S["mm_chunk"], NCHUNK * t + 4)
                if t >= 1:
                    act.wait_ge(S["qk_scaled"], t)
                nc.scalar.activation(sq_t, flat[:, 0:1024], ACT.Square).then_inc(S["qk_sq"], 1)
                act.wait_ge(S["mm_chunk"], NCHUNK * t + 5)
                if t >= 2:
                    act.wait_ge(kv_st[s], 32 * (t // 2))
                nc.scalar.activation(v_t[:, s, :], bank[:, 2, :], ACT.Copy).then_inc(S["v_done"], 1)
            evac_post(NT - 1)
            join(act, 2)

            act.sem_inc(S["sig_done"], 2)
            act.sem_inc(S["at_sb"], 2)
            act.sem_inc(S["s_sig"], 1)
            act.sem_inc(S["kt_act"], 1)
            act.wait_ge(S["qbd_done"], 1)

            def sigmoids(i, u):
                K = (u % NTP + 1) * P
                U = i * RU + u
                h = 4 * i + u // NTP
                act.wait_ge(S["qk_mm"], U + 1)
                act.wait_ge(S["scan_done"], U + 1)
                z0 = (place(u) % 2) * 1024
                z = flat[:, z0:z0 + K]
                settle(act)
                nc.scalar.activation(keep[:, u % 2, 0:K], z, ACT.Sigmoid, scale=-(HD ** -0.5),
                                     bias=nbb[:, bass.ds(h, 1)]).then_inc(S["keep_done"], 1)
                act.wait_ge(S["at_ps"], U + 1)
                settle(act)
                nc.scalar.activation(sig[:, u % 2, 0:K], z, ACT.Sigmoid, scale=HD ** -0.5,
                                     bias=bb[:, bass.ds(h, 1)]).then_inc(S["sig_done"], 1)

            def evac_aT(i, u):
                K = (u % NTP + 1) * P
                U = i * RU + u
                act.wait_ge(S["at_ps"], U + 3)
                act.wait_ge(S["pv_mm"], U + UNITS + 1)
                nc.scalar.activation(aT[:, u % 2, 0:K], flat[:, 2048:2048 + K], ACT.Copy).then_inc(S["at_sb"], 1)

            def sigmoids_s(i, r):
                b = RSEQ * i + r
                act.wait_ge(S["s_mm"], b + 2)
                act.wait_ge(S["s_scan"], b + 1)
                z0 = (place_s(r) % 2) * 1024
                for c0, z in ((0, flat[0:NS, z0:z0 + PAST]), (PAST, bank[0:NS, 7, 0:DS])):
                    n = z.shape[1]
                    nc.scalar.activation(keep_s[:, c0:c0 + n], z, ACT.Sigmoid, scale=-(HD ** -0.5), bias=nbs[:, :])\
                        .then_inc(S["s_keep"], 1)
                act.wait_ge(S["s_at"], b + 1)
                nc.scalar.activation(sig_s[:, PAST:], bank[0:NS, 7, 0:DS], ACT.Sigmoid, scale=HD ** -0.5,
                                     bias=bs[:, :]).then_inc(S["s_sig_new"], 1)
                nc.scalar.activation(sig_s[:, 0:PAST], flat[0:NS, z0:z0 + PAST], ACT.Sigmoid, scale=HD ** -0.5,
                                     bias=bs[:, :]).then_inc(S["s_sig"], 1)

            def stage_q(i, r):
                b = RSEQ * i + r
                act.wait_ge(S["s_mm"], b + 1)
                settle(act)
                nc.scalar.activation(q_stage[:, :, :], q_bd[:, bass.ds(b, 1), :, :].rearrange("p a c n -> p (a c) n"),
                                     ACT.Copy).then_inc(S["q_staged"], 1)
                nc.scalar.activation(kT[:, :, PAST:], kTs[:, :, bass.ds(b * DS, DS)], ACT.Copy)\
                    .then_inc(S["q_staged"], 1)

            def evac_o_all(i, r):
                b = RSEQ * i + r
                act.wait_ge(S["s_pv"], b + 2)
                nc.scalar.activation(o_all, bank[0:NS, 7, :], ACT.Copy).then_inc(S["s_o_all"], 1)

            def keys_act(i, u):
                b, g = RSEQ * i + u // SU, odd_page(u)
                act.wait_ge(S["kt_odd"], 4 * b + g // 2 + 1 + 4)
                if g == 1:
                    act.wait_ge(S["s_mm"], b + 1)
                nc.scalar.activation(kT[:, :, g * P:(g + 1) * P],
                                     bank[:, 2 * (place(u) % 2) + 1, :].rearrange("p (c n) -> p c n", c=NPAIR),
                                     ACT.Copy).then_inc(S["kt_act"], 1)

            with act.Fori(0, ROUNDS) as i:
                sigmoids(i, 0)
                keys_act(i, 0)
                for u in range(RU):
                    r, j = u // SU, u % SU
                    if j == S_AT - 1:
                        sigmoids_s(i, r)
                    if u + 1 < RU:
                        sigmoids(i, u + 1)
                        if odd_page(u + 1) is not None:
                            keys_act(i, u + 1)
                    if j == 1:
                        stage_q(i, r)
                    evac_aT(i, u)
                    if j == SU - 1:
                        evac_o_all(i, r)
            join(act, 3)

            def ln_square(j):
                c0, n = LN_COLS[j]
                act.wait_ge(S["ln_cent"], j + 1)
                if j >= 1:
                    act.wait_ge(S["ln_var"], j)
                nc.scalar.activation(ln_a[:, :, 0:n], cvT[:, :, c0:c0 + n], ACT.Square).then_inc(S["ln_sq"], 1)

            def ln_root(j):
                c0, n = LN_COLS[j]
                act.wait_ge(S["ln_dv"], j + 1)
                nc.scalar.activation(ln_v[:, 0:n], ln_v[:, 0:n], ACT.Sqrt).then_inc(S["ln_std"], 1)
                act.wait_ge(S["ln_norm"], j + 1)
                if j >= 1:
                    act.wait_ge(S["ln_done"], j)
                for ch in range(NCH):
                    nc.scalar.activation(ln_b[:, ch, 0:n], cvT[:, ch, c0:c0 + n], ACT.Sigmoid,
                                         scale=cw[:, ch, CW + 1:CW + 2], bias=cw[:, ch, CW + 2:CW + 3])\
                        .then_inc(S["ln_sig"], 1)

            def router_out(t):
                n = P if t < NTP else NS
                act.wait_ge(S["lg_mm"], t + 1)
                nc.scalar.activation(lgT[:, t * P:t * P + n], bank[0:E, 6, 0:n], ACT.Copy).then_inc(S["lg_sb"], 1)

            ln_square(0)
            ln_root(0)
            for t in range(NT):
                s = t % 2
                n = P if t < NTP else NS
                act.wait_ge(S["x1_done"], t + 1)
                if t >= 1:
                    act.wait_ge(S["x2_var"], t)
                    act.wait_ge(S["x2_sq"], t)
                nc.scalar.activation(sqx[0:n, :], x1[0:n, t, :], ACT.Square, accum_out=st[0:n, 4:5])\
                    .then_inc(S["x2_sq"], 1)
                if t >= 1:
                    router_out(t - 1)
                act.wait_ge(S["h2_ps"], t + 1)
                if t >= 2:
                    act.wait_ge(S["lg_mm"], t - 1)
                for j in range(2):
                    nc.scalar.activation(h2T[:, s, 4 * j:4 * j + 4, :],
                                         bank[:, 4 + j, :].rearrange("p (k n) -> p k n", k=4), ACT.Copy)\
                        .then_inc(S["h2T_sb"], 1)
                for j, at in LN_AT.items():
                    if t == at:
                        ln_square(j)
                    if t == at + 1:
                        ln_root(j)
            router_out(NT - 1)
            join(act, 4)
            act.wait_ge(S["r_m"], 1)
            nc.scalar.activation(r_e, r_z, ACT.Exp).then_inc(S["exp_ready"], 1)
            act.wait_ge(S["tiles_ready"], 1)
            pairs_used = act.value_load(n_pairs[0:1, 0:1], min_val=1, max_val=MT // 2)

            act.sem_inc(S["xgT_sb"], 1)
            act.sem_inc(S["g_sig"], 2)
            act.sem_inc(S["y_lo"], 1)

            def swish_gate(i, s):
                t = 2 * i + s
                act.wait_ge(S["gu_mm"], t + 3)
                act.wait_ge(S["aT_ps"], t + 1)
                nc.scalar.activation(act_t[:, s, :], bank[:, 2 * s, :], ACT.Sigmoid).then_inc(S["g_sig"], 1)

            def out_lo(i, s):
                t = 2 * i + s
                act.wait_ge(S["y_mm"], 2 * t + 5)
                act.wait_ge(y_st[s], 16 * i + 16)
                nc.scalar.activation(y_t[:, s, 0:512], bank[:, 6, :], ACT.Copy).then_inc(S["y_lo"], 1)

            def store_y(i, s):
                t = 2 * i + s
                act.wait_ge(S["y_lo"], t + 2)
                act.wait_ge(S["y_hi"], t + 2)
                act.dma_start(y_d[bass.ds(t * P, P), :], y_t[:, s, :]).then_inc(y_st[s], 16)

            def turned_lo(t, s):
                act.wait_ge(S["xg_ps"], t + 3)
                act.wait_ge(S["gu_mm"], t + 1)
                nc.scalar.activation(xgT[:, s, 0:4, :],
                                     bank[:, 4, :].rearrange("p (k n) -> p k n", k=4), ACT.Copy)\
                    .then_inc(S["xgT_sb"], 1)

            for s in range(2):
                act.sem_inc(y_st[s], 16)
            turned_lo(0, 0)
            with act.Fori(0, MT // 2) as i, act.If(i < pairs_used):
                turned_lo(2 * i + 1, 1)
                swish_gate(i, 0)
                swish_gate(i, 1)
                out_lo(i, 0)
                store_y(i, 0)
                out_lo(i, 1)
                turned_lo(2 * i + 2, 0)
                store_y(i, 1)
            for s in range(2):
                act.wait_ge(y_st[s], 16 * pairs_used + 16)
            settle(act)
            join(act, 5)

            for t in range(NT):
                n = P if t < NTP else NS
                act.wait_ge(ya_in[t], 32)
                nc.scalar.activation(ya[0:n, t, :], ya[0:n, t, :], ACT.Copy, scale=wgt[0:n, 0, t:t + 1])\
                    .then_inc(S["y_first"], 1)

        @block.tensor
        def _(pe):
            pe.sem_inc(S["ada_used"], 4)
            pe.wait_ge(S["pool_const"], 1)
            pe.wait_ge(S["c_silu"], 1)
            for k in range(KD):
                mm = pe.transpose(bank[:, 0, k * 16:k * 16 + 1 + DB], c9[:, k * P:(k + 1) * P],
                                  identf[0:1 + DB, 0:1 + DB])
            mm.then_inc(S["cT_ps"], 1)
            for ch in range(NCH):
                pe.transpose(bank[:, 1, ch * 64:ch * 64 + CW + 3], xt[0:CW + 3, 0, ch * P:(ch + 1) * P],
                             identf[0:CW + 3, 0:CW + 3])
            for j in range(2):
                for ch in range(NCH):
                    mm = pe.transpose(bank[:, 4 + j, ch * 120:(ch + 1) * 120],
                                      xt[0:120, 1, j * CC + ch * P:j * CC + (ch + 1) * P], identf[0:120, 0:120])
            mm.then_inc(S["st_ps"], 1)
            pe.wait_ge(S["cT_sb"], 1)
            with pe.Fori(0, NADA) as i:
                for cc in range(2):
                    pe.wait_ge(S["rows_done"], 2 * i + cc + 1)
                    for k in range(KD):
                        s = 2 * cc + k // 4
                        if k % 4 == 0:
                            pe.wait_ge(ada_in[s], 16 * i + 16)
                        mm = pe.matmul(bank[0:1 + DB, 2 + cc, :], cT[:, k, 0:1 + DB], ada[:, s, k % 4, :],
                                       start=(k == 0), stop=(k == KD - 1))
                        if k % 4 == 3:
                            mm.then_inc(S["ada_used"], 1)
            join(pe, 1)

            def turn_h(t):
                pe.wait_ge(S["h_ready"], t + 1)
                if t >= 1:
                    pe.wait_ge(S["hT_sb"], 2 * t)
                if t >= 2:
                    pe.wait_ge(S["q_sb"], t - 1)
                    pe.wait_ge(S["k_sb"], t - 1)
                for k in range(KD):
                    mm = pe.transpose(bank[:, 5 + k // 4, (k % 4) * P:(k % 4 + 1) * P],
                                      hrow[:, t % 2, k * P:(k + 1) * P], identf[:, :])
                mm.then_inc(S["hT_ps"], 1)

            def turn_post(t):
                s = t % 2
                pe.wait_ge(S["glu_done"], t + 1)
                if t >= 1:
                    pe.wait_ge(S["glu_sb"], t)
                for ch in range(NCH):
                    mm = pe.transpose(bank[:, 7, ch * P:(ch + 1) * P], glu_t[:, s, ch * P:(ch + 1) * P], identf[:, :])
                mm.then_inc(S["post_ps"], 1)
                pe.wait_ge(S["qk_done"], t + 1)
                pe.wait_ge(S["hT_sb"], min(2 * (t + 2), 2 * NT))
                for j in range(2):
                    for p in range(NPAIR):
                        mm = pe.transpose(bank[:, 5 + j, p * P:(p + 1) * P],
                                          qk_t[:, s, j * AW + p * P:j * AW + (p + 1) * P], identf[:, :])
                    mm.then_inc(S["post_ps"], 1)

            turn_h(0)
            for t in range(NT):
                s = t % 2
                pe.wait_ge(S["hT_sb"], 2 * (t + 1))
                for n, (cc, freed) in enumerate(zip(CHUNKS, ("glu_done", "glu_done", "qk_scaled", "qk_scaled",
                                                             "v_done"))):
                    if t == 0:
                        pe.wait_ge(w_in_in[cc], 16)
                    if t >= 1:
                        pe.wait_ge(S[freed], t)
                        if cc < 2:
                            pe.wait_ge(S["qk_sq"], t)
                        if cc == 4:
                            pe.wait_ge(S["sg_done"], t)
                    for k in range(KD):
                        mm = pe.matmul(bank[:, cc, :], hT[:, s, k, :], w_in_sb[:, k, cc * 512:(cc + 1) * 512],
                                       start=(k == 0), stop=(k == KD - 1))
                    mm.then_inc(S["mm_chunk"], 1)
                    if n == 1 and t >= 1:
                        turn_post(t - 1)
                    if n == 2 and t + 1 < NT:
                        turn_h(t + 1)
            turn_post(NT - 1)
            join(pe, 2)

            pe.sem_inc(S["at_ps"], 2)
            pe.sem_inc(S["pv_mm"], 2 + UNITS)
            pe.sem_inc(S["kt_even"], 4)
            pe.sem_inc(S["kt_odd"], 4)
            pe.sem_inc(S["s_pv"], 1)
            pe.sem_inc(S["s_mm"], 1)
            pe.sem_inc(S["s_at"], 1)

            def scores(i, u):
                s, hh, qb = u // UNITS, (u // NTP) % 2, u % NTP
                U = i * RU + u
                if u % UNITS == 0:
                    pe.wait_ge(stage_in[s], 48 * i + 48)
                pe.wait_ge(S["sig_done"], U + 1)
                if u % SU in (SU // 2, SU // 2 + 1):
                    pe.wait_ge(S["kt_act"], 4 * (RSEQ * i + u // SU) + u % SU)
                if u % SU == S_AT:
                    pe.wait_ge(S["sig_done"], U + 2)
                if u % SU == S_AT + 1:
                    pe.wait_ge(S["s_sig"], RSEQ * i + u // SU + 2)
                z0 = 2 * (place(u) % 2)
                K = (qb + 1) * P
                pp = slice(64 * hh, 64 * hh + 64)
                for c0 in range(0, K, 512):
                    n = min(512, K - c0)
                    pe.matmul(bank[:, z0 + c0 // 512, 0:n], stage[pp, s, 0, qb * P:(qb + 1) * P],
                              stage[pp, s, 1, c0:c0 + n], start=True, stop=c0 + n < K)
                k0 = qb * P % 512
                mm = pe.matmul(bank[:, z0 + qb // 4, k0:k0 + P], identb[:, :], causal[:, :],
                               start=False, stop=True)
                mm.then_inc(S["qk_mm"], 1)

            def turn_a(i, u):
                U = i * RU + u
                pe.wait_ge(S["a_done"], U + 1)
                pe.wait_ge(S["at_sb"], U + 2)
                for kb in range(u % NTP + 1):
                    mm = pe.transpose(bank[:, 4 + kb // 4, (kb % 4) * P:(kb % 4 + 1) * P],
                                      sig[:, u % 2, kb * P:(kb + 1) * P], identf[:, :])
                mm.then_inc(S["at_ps"], 1)

            def values(i, u):
                s, hh, qb = u // UNITS, (u // NTP) % 2, u % NTP
                U = i * RU + u
                pe.wait_ge(S["at_sb"], U + 3)
                if u % 4 == 0:
                    pe.wait_ge(S["o_sb"], i * (RU // 4) + u // 4 + 1)
                ob = bank[64 * hh:64 * hh + 64, 6, (qb % 4) * P:(qb % 4 + 1) * P]
                for kb in range(qb + 1):
                    mm = pe.matmul(ob, stage[:, s, 2, kb * P + 64 * hh:kb * P + 64 * hh + 64],
                                   aT[:, u % 2, kb * P:(kb + 1) * P], start=(kb == 0), stop=(kb == qb))
                mm.then_inc(S["pv_mm"], 1)

            def turn_keys(i, u, g):
                b = RSEQ * i + u // SU
                pe.wait_ge(k_in[g], 16 * b + 16)
                if g == 0:
                    pe.wait_ge(S["s_o"], 2 * b + 1)
                elif g % 2 == 0:
                    pe.wait_ge(S["kt_dve"], 4 * b + g // 2 + 1)
                elif g > 4:
                    pe.wait_ge(S["kt_act"], 4 * b + g // 2)
                kb = 7 if g % 2 == 0 else 2 * (place(u) % 2) + 1
                for p in range(NPAIR):
                    mm = pe.transpose(bank[:, kb, p * P:(p + 1) * P], k_pg[g][:, p * P:(p + 1) * P],
                                      identf[:, :])
                mm.then_inc(S[("kt_even", "kt_odd")[g % 2]], 1)

            def scores_s(i, r):
                b = RSEQ * i + r
                pe.wait_ge(S["kt_act"], 4 * b + 5)
                pe.wait_ge(S["kt_dve"], 4 * b + 5)
                pe.wait_ge(S["q_staged"], 2 * b + 2)
                pe.wait_ge(S["sig_done"], RU * i + r * SU + S_AT + 1)
                z0 = 2 * (place_s(r) % 2)
                for c0 in range(0, PAST, 512):
                    for p in range(NPAIR):
                        pe.matmul(bank[0:NS, z0 + c0 // 512, :], q_stage[:, p, :], kT[:, p, c0:c0 + 512],
                                  start=(p == 0), stop=(p == NPAIR - 1))
                for p in range(NPAIR):
                    pe.matmul(bank[0:NS, 7, 0:DS], q_stage[:, p, :], kT[:, p, PAST:], start=(p == 0), stop=False)
                mm = pe.matmul(bank[0:NS, 7, 0:DS], q_of_row[:, :, :].rearrange("p h i -> p (h i)"),
                               causal[0:DS, 0:DS], start=False, stop=True)
                mm.then_inc(S["s_mm"], 1)

            def turn_a_s(i, r):
                b = RSEQ * i + r
                pe.wait_ge(S["s_a"], b + 1)
                settle(pe)
                for g in range(NPG):
                    pe.transpose(bank[:, 7, g * NS:(g + 1) * NS], sig_s[:, g * P:(g + 1) * P], identf[0:NS, 0:NS])
                pe.transpose(bank[0:DS, 7, NPG * NS:(NPG + 1) * NS], sig_s[:, PAST:PAST + DS], identf[0:NS, 0:NS])\
                    .then_inc(S["s_at"], 1)

            def values_s(i, r):
                b = RSEQ * i + r
                pe.wait_ge(S["v_in"], 16 * (NPG + 1) * b + 16 * (NPG + 1))
                pe.wait_ge(S["s_at_sb"], 2 * b + 2)
                settle(pe)
                for g in range(NPG):
                    pe.matmul(bank[0:NS, 7, :], aT_s[:, g, :], v_pg[:, g, :], start=(g == 0), stop=False)
                pe.matmul(bank[0:NS, 7, :], aT_s[0:DS, NPG, :], v_new, start=False, stop=True)\
                    .then_inc(S["s_pv"], 1)

            def turn_o_s(i, r):
                pe.wait_ge(S["s_o_all"], RSEQ * i + r + 1)
                settle(pe)
                for p in range(NPAIR):
                    mm = pe.transpose(bank[:, 7, p * NS:(p + 1) * NS], o_all[:, p * P:(p + 1) * P],
                                      identf[0:NS, 0:NS])
                mm.then_inc(S["s_o_ps"], 1)

            with pe.Fori(0, ROUNDS) as i:
                scores(i, 0)
                turn_keys(i, 0, odd_page(0))
                for u in range(RU):
                    r, j = u // SU, u % SU
                    if j == S_AT - 1:
                        scores_s(i, r)
                    if u + 1 < RU:
                        scores(i, u + 1)
                        if odd_page(u + 1) is not None:
                            turn_keys(i, u + 1, odd_page(u + 1))
                    if even_page(u) is not None:
                        turn_keys(i, u, even_page(u))
                    if j == SU - 1:
                        turn_a_s(i, r)
                    if j == 0 and r >= 1:
                        turn_o_s(i, r - 1)
                    turn_a(i, u)
                    if u >= 1:
                        values(i, u - 1)
                    if j == SU - 1:
                        values_s(i, r)
                values(i, RU - 1)
                turn_o_s(i, RSEQ - 1)
            join(pe, 3)

            def mix(t, part):
                n = P if t < NTP else NS
                if t >= 2 and part == 0:
                    pe.wait_ge(S["x1_tmp"], t - 1)
                if part == 1:
                    pe.wait_ge(S["ln_done"], t // 4 + 1)
                for cc in range(2):
                    for k in range(part * NPAIR, (part + 1) * NPAIR):
                        if t == 0 and cc == 0:
                            pe.wait_ge(S[("w_attn_in", "w_conv_in")[part]], 16 * NPAIR)
                        cat = oT if part == 0 else cvT
                        mm = pe.matmul(bank[0:n, 2 * (t % 2) + cc, :], cat[:, k % NPAIR, t * P:t * P + n],
                                       w_out_sb[:, k, cc * 512:(cc + 1) * 512], start=(k == 0), stop=(k == KD - 1))
                if part == 1:
                    mm.then_inc(S["mix_mm"], 1)

            def ln_mean(j):
                c0, n = LN_COLS[j]
                if j >= 1:
                    pe.wait_ge(S["ln_dv"], j)
                for ch in range(NCH):
                    mm = pe.matmul(bank[:, 7, 0:n], mean_of[:, :], cvT[:, ch, c0:c0 + n],
                                   start=(ch == 0), stop=(ch == NCH - 1))
                mm.then_inc(S["ln_mean"], 1)

            def ln_var(j):
                c0, n = LN_COLS[j]
                pe.wait_ge(S["ln_sq"], j + 1)
                for ch in range(NCH):
                    mm = pe.matmul(bank[:, 7, 0:n], mean_of[:, :], ln_a[:, ch, 0:n],
                                   start=(ch == 0), stop=(ch == NCH - 1))
                mm.then_inc(S["ln_var"], 1)

            def route(t):
                n = P if t < NTP else NS
                pe.wait_ge(S["h2_done"], t + 1)
                if t >= 1:
                    pe.wait_ge(S["h2T_sb"], 2 * t)
                for k in range(KD):
                    mm = pe.transpose(bank[:, 4 + k // 4, (k % 4) * P:(k % 4) * P + n],
                                      h2[0:n, t % 2, k * P:(k + 1) * P], identf[0:n, 0:n])
                mm.then_inc(S["h2_ps"], 1)

            def router(t):
                n = P if t < NTP else NS
                pe.wait_ge(S["h2T_sb"], 2 * t + 2)
                if t >= 1:
                    pe.wait_ge(S["lg_sb"], t)
                for k in range(KD):
                    mm = pe.matmul(bank[0:E, 6, 0:n], wr[:, k, :], h2T[:, t % 2, k, 0:n],
                                   start=(k == 0), stop=(k == KD - 1))
                mm.then_inc(S["lg_mm"], 1)

            ln_mean(0)
            ln_var(0)
            mix(0, 0)
            mix(1, 0)
            mix(0, 1)
            for t in range(NT):
                if t + 1 < NT:
                    mix(t + 1, 1)
                for j, at in LN_AT.items():
                    if t == at:
                        ln_mean(j)
                    if t == at + 1:
                        ln_var(j)
                if t + 2 < NT:
                    mix(t + 2, 0)
                if t >= 1:
                    router(t - 1)
                route(t)
            router(NT - 1)
            pe.wait_ge(S["lg_sb"], NT)
            for t in range(NT):
                n = P if t < NTP else NS
                pe.transpose(bank[0:n, 7, t * E:(t + 1) * E], lgT[:, t * P:t * P + n], identf[0:E, 0:E])
            join(pe, 4)
            pe.wait_ge(S["r_ready"], 1)
            pe.matmul(bank[:, 0, 0:NT * E], before[:, :], r_maskb, start=True, stop=True)
            pe.matmul(bank[:, 1, 0:NT * E], onesb[:, :], r_maskb, start=True, stop=True).then_inc(S["r_m"], 1)
            pe.sem_inc(S["gu_mm"], 2)
            pe.sem_inc(S["y_mm"], 4)
            pe.wait_ge(S["r_ready"], 2)
            for a in range(2 * NT):
                mm = pe.matmul(bank[:, 2, 0:2 * MT], at_row[:, a, :], tile_id[:, a, :, :].rearrange("p w n -> p (w n)"),
                               start=(a == 0), stop=(a == 2 * NT - 1))
            mm.then_inc(S["r_m"], 1)
            pe.wait_ge(S["tiles_ready"], 1)
            pairs_used = pe.value_load(n_pairs[0:1, 0:1], min_val=1, max_val=MT // 2)

            pe.sem_inc(S["xg_ps"], 2)
            pe.sem_inc(S["aT_ps"], 2)

            def turn_x(t, s, nth, acts):
                pe.wait_ge(xg_in[s], 16 * nth)
                pe.wait_ge(S["xgT_sb"], t + 1)
                pe.wait_ge(S["xgT_hi"], t + 1)
                pe.wait_ge(S["aT_sb"], acts + 1)
                for k in range(KD):
                    mm = pe.transpose(bank[:, 4 + k // 4, (k % 4) * P:(k % 4 + 1) * P],
                                      xg[:, s, k * P:(k + 1) * P], identf[:, :])
                mm.then_inc(S["xg_ps"], 1)

            def gate_or_up(i, s, w):
                t = 2 * i + s
                if w == 0:
                    pe.wait_ge(S["xgT_sb"], t + 2)
                    pe.wait_ge(S["xgT_hi"], t + 2)
                    pe.wait_ge(S["g_sig"], t + 1)
                    pe.wait_ge(S["act_done"], t + 1)
                w_sb, arrived = ((wg_sb, wg_in), (wu_sb, wu_in))[w]
                pe.wait_ge(arrived[s], 16 * i + 16)
                for k in range(KD):
                    mm = pe.matmul(bank[:, 2 * s + w, :], xgT[:, s, k, :], w_sb[:, s, k, :],
                                   start=(k == 0), stop=(k == KD - 1))
                if w == 1:
                    mm.then_inc(S["gu_mm"], 1)

            def turn_act(i, s):
                t = 2 * i + s
                pe.wait_ge(S["act_done"], t + 3)
                pe.wait_ge(S["aT_sb"], t + 1)
                for k in range(KF):
                    mm = pe.transpose(bank[:, 4, k * P:(k + 1) * P], act_t[:, s, k * P:(k + 1) * P], identf[:, :])
                mm.then_inc(S["aT_ps"], 1)

            def down(i, s, w):
                t = 2 * i + s
                if w == 0:
                    pe.wait_ge(S["aT_sb"], t + 2)
                    pe.wait_ge(wd_in[s], 16 * i + 16)
                pe.wait_ge(S["y_lo" if w == 0 else "y_hi"], t + 1)
                for k in range(KF):
                    mm = pe.matmul(bank[:, 6 + w, :], actT[:, s, k, :], wd_sb[:, s, k, w * 512:(w + 1) * 512],
                                   start=(k == 0), stop=(k == KF - 1))
                mm.then_inc(S["y_mm"], 1)

            turn_x(0, 0, 1, 0)
            with pe.Fori(0, MT // 2) as i, pe.If(i < pairs_used):
                gate_or_up(i, 0, 0)
                turn_x(2 * i + 1, 1, i + 1, 2 * i)
                gate_or_up(i, 0, 1)
                gate_or_up(i, 1, 0)
                turn_act(i, 0)
                gate_or_up(i, 1, 1)
                down(i, 0, 0)
                turn_act(i, 1)
                down(i, 0, 1)
                down(i, 1, 0)
                turn_x(2 * i + 2, 0, i + 2, 2 * i + 2)
                down(i, 1, 1)
            join(pe, 5)

        @block.vector
        def _(dve):
            c = Chain(dve, S["dve_c"])
            V = nc.vector
            dve.sem_inc(S["rows_done"], 2)
            dve.wait_ge(S["c_sig"], 1)
            V.tensor_tensor(c9, c9, csig, ALU.mult).then_inc(S["c_silu"], 1)
            with dve.Fori(0, NADA) as i:
                for cc in range(2):
                    dve.wait_ge(S["ada_used"], 4 * i + 2 * cc + 6)
                    dve.wait_ge(S["brow_in"], 16 * i + 16)
                    dve.wait_ge(S["rows_stored"], 16 * i + 16)
                    V.tensor_tensor(mrow[:, cc * 512:(cc + 1) * 512], bank[0:1 + DB, 2 + cc, :],
                                    brow[:, cc * 512:(cc + 1) * 512], ALU.add).then_inc(S["rows_done"], 1)
            dve.wait_ge(S["mod1_in"], 16 * 5)
            for kind, n in ((0, P), (1, NS)):
                c.put(V.scalar_tensor_tensor(AB[0:n, kind, 0, :], AB[0:n, kind, 0, :], 1.0, hrow[0:n, 0, :],
                                             ALU.add, ALU.mult))
            c.wait()
            join(dve, 1)

            def var_x(t):
                dve.wait_ge(S["x_sq"], t + 1)
                s = t % 2
                if t >= 2:
                    dve.wait_ge(S["x_rstd"], t - 1)
                V.tensor_scalar(st[:, s:s + 1], st[:, 4 + s:5 + s], 1.0 / D, EPS, ALU.mult, ALU.add)\
                    .then_inc(S["x_var"], 1)

            def norm_x(t):
                s = t % 2
                n, kind = (P, 0) if t < NTP else (NS, 1)
                dve.wait_ge(S["x_rstd"], t + 1)
                c.put(V.scalar_tensor_tensor(hrow[0:n, s, :], xt[0:n, s, :], st[0:n, 2 + s:3 + s],
                                             AB[0:n, kind, 0, :], ALU.mult, ALU.mult))
                c.wait()
                V.tensor_tensor(hrow[0:n, s, :], hrow[0:n, s, :], AB[0:n, kind, 1, :], ALU.add)\
                    .then_inc(S["h_ready"], 1)

            def conv_taps(pair, chs, t0, t1):
                n0 = pair * 2 * P
                if t0 == 0:
                    dve.wait_ge(S["glu_sb"], 2 * pair + 2)
                for tap in range(t0, t1):
                    for ch in chs:
                        out = cvT[:, ch, n0:n0 + 2 * P]
                        src = glu_x[:, ch, n0 + tap:n0 + tap + 2 * P]
                        if tap == 0:
                            c.put(V.tensor_scalar(out, src, cw[:, ch, 0:1], cw[:, ch, CW:CW + 1], ALU.mult, ALU.add))
                        else:
                            c.wait(back=len(chs) - 1)
                            c.put(V.scalar_tensor_tensor(out, src, cw[:, ch, tap:tap + 1], out, ALU.mult, ALU.add))

            def conv_part(t, part):
                j = t - 2
                if 0 <= j < NTP - 2:
                    chs = (0, 1) if j % 2 == 0 else (2, 3)
                    conv_taps(j // 2, chs, (0, 8, 16, 24)[part], (8, 16, 24, CW)[part])

            dve.wait_ge(S["st_sb"], 1)
            var_x(0)
            norm_x(0)
            var_x(1)
            norm_x(1)
            for t in range(NT):
                s = t % 2
                dve.wait_ge(S["sg_done"], t + 1)
                dve.wait_ge(S["mm_chunk"], NCHUNK * t + 2)
                if t >= 2:
                    dve.wait_ge(S["post_ps"], 3 * (t - 2) + 1)
                if t == NTP + 1:
                    dve.wait_ge(S["conv_st"], 16)
                V.tensor_tensor(glu_t[:, s, :], bank[:, 3, :], sg_t[:, s, :], ALU.mult).then_inc(S["glu_done"], 1)
                conv_part(t, 0)
                dve.wait_ge(S["qk_sq"], t + 1)
                c.wait()
                c.put(V.tensor_reduce(st[:, 48:64], sq_t.rearrange("p (h d) -> p h d", d=HD), AX_X, ALU.add))
                c.wait()
                if t >= 1:
                    dve.wait_ge(S["qk_rstd"], t)
                V.tensor_scalar(st[:, 16:32], st[:, 48:64], 1.0 / HD, EPS, ALU.mult, ALU.add)\
                    .then_inc(S["qk_var"], 1)
                conv_part(t, 1)
                dve.wait_ge(S["qk_rstd"], t + 1)
                if t >= 2:
                    dve.wait_ge(S["post_ps"], 3 * (t - 2) + 3)
                    dve.wait_ge(kv_st[s], 32 * (t // 2))
                V.tensor_tensor(qk_t[:, s, :].rearrange("p (h d) -> p h d", d=HD),
                                flat[:, 0:1024].rearrange("p (h d) -> p h d", d=HD),
                                st[:, 32:48].unsqueeze(2).broadcast_to([P, 16, HD]), ALU.mult)\
                    .then_inc(S["qk_scaled"], 1)
                conv_part(t, 2)
                if t + 2 < NT:
                    var_x(t + 2)
                    norm_x(t + 2)
                conv_part(t, 3)
            c.wait()
            join(dve, 2)

            dve.sem_inc(S["scan_done"], 2)
            dve.sem_inc(S["o_sb"], 1)
            dve.sem_inc(S["kt_dve"], 1)
            dve.sem_inc(S["s_scan"], 1)
            dve.sem_inc(S["s_o"], 1)
            for s in range(2):
                c.put(V.memset(prod[:, s, 1024:1025], 1.0))
            c.put(V.memset(xt[:, 0, :], 0.0))
            c.put(V.memset(prod_s[:, KN:KN + 1], 1.0))
            c.wait()
            for h in range(H):
                pp = slice(64 * (h % 2), 64 * (h % 2) + 64)
                c.put(V.tensor_copy(q_bd[pp, :, h // 2, h * DS:(h + 1) * DS],
                                    qTs[pp, h // 2, :].rearrange("p (b n) -> p b n", b=DB)))
            c.wait()
            dve.sem_inc(S["qbd_done"], 1)
            c.reset()

            def stick(i, u, evac=None):
                K = (u % NTP + 1) * P
                U = i * RU + u
                dve.wait_ge(S["keep_done"], U + 1)
                kept = prod[:, u % 2, 1024 - K:1024]
                V.tensor_tensor_scan(kept[:, ::-1], keep[:, u % 2, 0:K][:, ::-1], keep[:, u % 2, 0:K][:, ::-1],
                                     1.0, ALU.mult, ALU.bypass).then_inc(S["scan_done"], 1)
                if evac is not None:
                    evac_o(i, evac)
                dve.wait_ge(S["sig_done"], U + 3)
                dve.wait_ge(S["scan_done"], U + 3)
                V.tensor_tensor(sig[:, u % 2, 0:K], sig[:, u % 2, 0:K], prod[:, u % 2, 1025 - K:1025], ALU.mult)\
                    .then_inc(S["a_done"], 1)

            def evac_o(i, g):
                pair = 2 * i + g // 4
                hh, half = (g // 2) % 2, g % 2
                dve.wait_ge(S["pv_mm"], i * RU + 4 * g + 4 + 2 + UNITS)
                pp = slice(64 * hh, 64 * hh + 64)
                V.tensor_copy(oT[pp, bass.ds(pair, 1), half * 512:(half + 1) * 512].rearrange("p a n -> p (a n)"),
                              bank[pp, 6, :]).then_inc(S["o_sb"], 1)

            def keys_dve(i, r, g):
                dve.wait_ge(S["kt_even"], 4 * (RSEQ * i + r) + g // 2 + 1 + 4)
                if g == 0:
                    dve.wait_ge(S["s_mm"], RSEQ * i + r + 1)
                V.tensor_copy(kT[:, :, g * P:(g + 1) * P],
                              bank[:, 7, :].rearrange("p (c n) -> p c n", c=NPAIR)).then_inc(S["kt_dve"], 1)

            def stick_s(i, r):
                b = RSEQ * i + r
                dve.wait_ge(S["s_keep"], 2 * b + 2)
                V.tensor_tensor_scan(prod_s[:, 0:KN][:, ::-1], keep_s[:, ::-1], keep_s[:, ::-1], 1.0,
                                     ALU.mult, ALU.bypass).then_inc(S["s_scan"], 1)
                dve.wait_ge(S["s_scan"], b + 2)
                dve.wait_ge(S["s_sig"], b + 2)
                dve.wait_ge(S["s_sig_new"], b + 1)
                V.tensor_tensor(sig_s, sig_s, prod_s[:, 1:KN + 1], ALU.mult).then_inc(S["s_a"], 1)

            def evac_a_s(i, r):
                b = RSEQ * i + r
                dve.wait_ge(S["s_at"], b + 2)
                dve.wait_ge(S["s_pv"], b + 1)
                V.tensor_copy(aT_s[:, 0:NPG, :], bank[:, 7, 0:NPG * NS].rearrange("p (g n) -> p g n", g=NPG))\
                    .then_inc(S["s_at_sb"], 1)
                V.tensor_copy(aT_s[0:DS, NPG, :], bank[0:DS, 7, NPG * NS:(NPG + 1) * NS])\
                    .then_inc(S["s_at_sb"], 1)

            def evac_o_s(i, r):
                b = RSEQ * i + r
                dve.wait_ge(S["s_o_ps"], b + 1)
                own = bank[:, 7, 0:NPAIR * (NS + 2 * DS)].rearrange("p (c n) -> p c n", c=NPAIR)
                for hh in range(2):
                    pp = slice(64 * hh, 64 * hh + 64)
                    V.tensor_copy(oT[pp, :, bass.ds(b * DS + SEQ, DS)], own[pp, :, DS * hh:DS * hh + DS])\
                        .then_inc(S["s_o"], 1)

            def conv_tap(i, tap):
                for cb in range(2):
                    ch = 2 * i + cb
                    w = cw[:, bass.ds(ch, 1), tap:tap + 1].rearrange("p a n -> p (a n)")
                    wb = cw[:, bass.ds(ch, 1), CW:CW + 1].rearrange("p a n -> p (a n)")
                    n0 = SEQ - 2 * P
                    x_last = glu_x[:, bass.ds(ch, 1), n0 + tap:SEQ + tap].rearrange("p a n -> p (a n)")
                    y_last = cvT[:, bass.ds(ch, 1), n0:SEQ].rearrange("p a n -> p (a n)")
                    x_smp = glu_s[:, bass.ds(ch, 1), :, tap:tap + DS].rearrange("p a b n -> p (a b) n")
                    y_smp = cvT[:, bass.ds(ch, 1), SEQ:TOK].rearrange("p a (b n) -> p (a b) n", b=DB)
                    for src, out in ((x_last, y_last), (x_smp, y_smp)):
                        if tap == 0:
                            c.put(V.tensor_scalar(out, src, w, wb, ALU.mult, ALU.add))
                        else:
                            c.wait(back=3)
                            c.put(V.scalar_tensor_tensor(out, src, w, out, ALU.mult, ALU.add))

            with dve.Fori(0, ROUNDS) as i:
                for u in range(RU):
                    r, j = u // SU, u % SU
                    stick(i, u, (u - 5) // 4 if u >= 5 and (u - 5) % 4 == 0 else None)
                    if j == S_AT:
                        stick_s(i, r)
                    if j == SU - 1:
                        evac_a_s(i, r)
                    if even_page(u) is not None:
                        keys_dve(i, r, even_page(u))
                    if j == 0 and r >= 1:
                        evac_o_s(i, r - 1)
                    for first in {S_AT - 1: (0,), SU - 1: (4,)}.get(j, ()):
                        for tap in range(8 * r + first, min(8 * r + first + 4, CW)):
                            conv_tap(i, tap)
                evac_o_s(i, RSEQ - 1)
                evac_o(i, RU // 4 - 1)
                c.reset()
            join(dve, 3)

            def ln_center(j):
                c0, n = LN_COLS[j]
                y = cvT[:, :, c0:c0 + n]
                dve.wait_ge(S["ln_mean"], j + 1)
                V.tensor_tensor(y, y, bank[:, 7, 0:n].unsqueeze(1).broadcast_to([P, NCH, n]), ALU.subtract)\
                    .then_inc(S["ln_cent"], 1)

            def ln_scale(j):
                c0, n = LN_COLS[j]
                y = cvT[:, :, c0:c0 + n]
                dve.wait_ge(S["ln_var"], j + 1)
                V.tensor_scalar(ln_v[:, 0:n], bank[:, 7, 0:n], EPS, None, ALU.add).then_inc(S["ln_dv"], 1)
                dve.wait_ge(S["ln_std"], j + 1)
                c.put(V.reciprocal(ln_r[:, 0:n], ln_v[:, 0:n]))
                c.wait()
                V.tensor_tensor(y, y, ln_r[:, 0:n].unsqueeze(1).broadcast_to([P, NCH, n]), ALU.mult)\
                    .then_inc(S["ln_norm"], 1)

            def ln_swish(j):
                c0, n = LN_COLS[j]
                y = cvT[:, :, c0:c0 + n]
                dve.wait_ge(S["ln_norm"], j + 1)
                dve.wait_ge(S["ln_sig"], NCH * (j + 1))
                for ch in range(NCH):
                    c.put(V.tensor_scalar(cvT[:, ch, c0:c0 + n], cvT[:, ch, c0:c0 + n], cw[:, ch, CW + 1:CW + 2],
                                          cw[:, ch, CW + 2:CW + 3], ALU.mult, ALU.add))
                c.wait()
                V.tensor_tensor(y, y, ln_b[:, :, 0:n], ALU.mult).then_inc(S["ln_done"], 1)

            ln_center(0)
            ln_scale(0)
            ln_swish(0)
            dve.wait_ge(S["mod2_in"], 16 * 9)
            for kind, n in ((0, P), (1, NS)):
                c.put(V.scalar_tensor_tensor(mod2[0:n, 1, kind, :], mod2[0:n, 1, kind, :], 1.0, gffn[0:n, :],
                                             ALU.add, ALU.mult))
            c.put(V.memset(logits[:, NTP, :], 0.0))
            c.put(V.tensor_copy(ramp[:, :], ramp_i[:, :]))
            c.wait()

            def gated(t):
                n, kind = (P, 0) if t < NTP else (NS, 1)
                dve.wait_ge(S["mix_mm"], t + 1)
                b0 = 1024 * (t % 2)
                V.tensor_tensor(x1[0:n, t, :], flat[0:n, b0:b0 + D], mod2[0:n, 0, kind, :], ALU.mult)\
                    .then_inc(S["x1_tmp"], 1)

            gated(0)
            for t in range(NT):
                s = t % 2
                n, kind = (P, 0) if t < NTP else (NS, 1)
                dve.wait_ge(S["x2_sq"], t + 1)
                if t >= 1:
                    dve.wait_ge(S["x2_rstd"], t)
                V.tensor_scalar(st[0:n, 0:1], st[0:n, 4:5], 1.0 / D, EPS, ALU.mult, ALU.add).then_inc(S["x2_var"], 1)
                dve.wait_ge(S["x2_rstd"], t + 1)
                if t >= 2:
                    dve.wait_ge(S["h2_ps"], t - 1)
                    dve.wait_ge(h2_stored[s], 16 * (t // 2))
                c.put(V.scalar_tensor_tensor(h2[0:n, s, :], x1[0:n, t, :], st[0:n, 2:3], mod2[0:n, 1, kind, :],
                                             ALU.mult, ALU.mult))
                c.wait()
                V.tensor_tensor(h2[0:n, s, :], h2[0:n, s, :], mod2[0:n, 2, kind, :], ALU.add)\
                    .then_inc(S["h2_done"], 1)
                if t + 1 < NT:
                    gated(t + 1)
                for j, at in LN_AT.items():
                    if t == at:
                        ln_center(j)
                    if t == at + 1:
                        ln_scale(j)
                    if t == at + 2:
                        ln_swish(j)
            join(dve, 4)

            def op(ins):
                c.put(ins)
                c.wait()

            def col(v, n):
                return v.unsqueeze(2).broadcast_to([P, NT, n])

            def row(v, n, m):
                return v.unsqueeze(1).broadcast_to([P, n, m])

            turned = bank[:, 7, 0:NT * E].rearrange("p (t e) -> p t e", e=E)
            c.put(V.tensor_copy(logits[:, 0:NTP, :], turned[:, 0:NTP, :]))
            op(V.tensor_copy(logits[0:NS, NTP, :], turned[0:NS, NTP, :]))
            op(V.tensor_reduce(r_a, logits[:, :, :], AX_X, ALU.max))
            op(V.tensor_tensor(r_z, logits[:, :, :], col(r_a, E), ALU.subtract))
            dve.sem_inc(S["r_m"], 1)
            op(V.memset(r_valid, 1.0))
            op(V.memset(r_valid[:, NTP, :], 0.0))
            op(V.memset(r_valid[0:NS, NTP, :], 1.0))
            op(V.tensor_copy(r_part, tok_part_i[:, :, :].rearrange("p w t -> p (w t)")))
            for w in range(2):
                c.put(V.tensor_tensor(r_part[:, w * NT:(w + 1) * NT], r_part[:, w * NT:(w + 1) * NT],
                                      r_valid[:, :, 0], ALU.mult))
            op(V.memset(slot_tok[:, MT:], 0))
            op(V.memset(r_base[:, 0, :], 0.0))
            dve.wait_ge(S["exp_ready"], 1)
            op(V.tensor_reduce(r_a, r_e, AX_X, ALU.add))
            op(V.reciprocal(r_b, r_a))
            op(V.tensor_tensor(r_p, r_e, col(r_b, E), ALU.mult))
            op(V.tensor_tensor(r_sel, r_p, row(br[:, :], NT, E), ALU.add))
            pairs = r_sel.rearrange("p t (g j) -> p (t g) j", j=2)
            op(V.tensor_tensor(r_hi, pairs[:, :, 0], pairs[:, :, 1], ALU.max))
            op(V.tensor_tensor(r_lo, pairs[:, :, 0], pairs[:, :, 1], ALU.min))
            hi2 = r_hi.rearrange("p (g j) -> p g j", j=2)
            lo2 = r_lo.rearrange("p (g j) -> p g j", j=2)
            op(V.tensor_tensor(r_gs, hi2[:, :, 0], hi2[:, :, 1], ALU.add))
            for j in range(2):
                op(V.tensor_tensor(r_g1, hi2[:, :, j], lo2[:, :, j], ALU.add))
                op(V.tensor_tensor(r_gs, r_gs, r_g1, ALU.max))
            gs = r_gs.rearrange("p (t g) -> p t g", g=EG)
            g1 = r_g1.rearrange("p (t g) -> p t g", g=EG)
            op(V.tensor_reduce(r_a, gs, AX_X, ALU.max))
            op(V.tensor_tensor(g1, gs, col(r_a, EG), ALU.is_equal))
            op(V.tensor_tensor(g1, g1, row(g_rank, NT, EG), ALU.mult))
            op(V.tensor_reduce(r_a, g1, AX_X, ALU.max))
            op(V.tensor_tensor(g1, g1, col(r_a, EG), ALU.is_equal))
            in_grp = r_g1.unsqueeze(2).broadcast_to([P, NT * EG, EPG])
            sel4 = r_sel.rearrange("p t (g j) -> p (t g) j", j=EPG)
            off4 = r_off.rearrange("p t (g j) -> p (t g) j", j=EPG)
            op(V.tensor_tensor(sel4, sel4, in_grp, ALU.mult))
            op(V.tensor_scalar(off4, in_grp, -NEG, NEG, ALU.mult, ALU.add))
            op(V.tensor_tensor(r_sel, r_sel, r_off, ALU.add))
            for j, hot in enumerate((r_h0, r_h1)):
                op(V.tensor_reduce(r_a, r_sel, AX_X, ALU.max))
                op(V.tensor_tensor(hot, r_sel, col(r_a, E), ALU.is_equal))
                op(V.tensor_tensor(hot, hot, row(e_rank, NT, E), ALU.mult))
                op(V.tensor_reduce(r_a, hot, AX_X, ALU.max))
                op(V.tensor_tensor(hot, hot, col(r_a, E), ALU.is_equal))
                if j == 0:
                    op(V.tensor_scalar(r_off, hot, 3.0 * NEG, None, ALU.mult))
                    op(V.tensor_tensor(r_sel, r_sel, r_off, ALU.add))
            op(V.tensor_tensor(r_off, r_h0, r_h1, ALU.add))
            op(V.tensor_tensor(r_mask3, r_off, r_valid, ALU.mult))
            dve.sem_inc(S["r_ready"], 1)
            dve.wait_ge(S["r_m"], 2)
            tot = bank[:, 1, 0:NT * E].rearrange("p (t e) -> p t e", e=E)
            for t in range(NT):
                op(V.tensor_tensor(r_base[:, t + 1, :], r_base[:, t, :], tot[:, t, :], ALU.add))
            caps = r_cmp[:, 0:E * NCAP].rearrange("p (e j) -> p e j", e=E)
            op(V.tensor_tensor(caps, r_base[:, NT, :].unsqueeze(2).broadcast_to([P, E, NCAP]),
                               row(cap_no, E, NCAP), ALU.is_gt))
            op(V.tensor_reduce(r_nt, caps, AX_X, ALU.add))
            op(V.tensor_tensor_scan(r_end, r_nt, r_nt, 0.0, ALU.add, ALU.bypass))
            ends = r_cmp.rearrange("p (t e) -> p t e", e=E)
            op(V.tensor_tensor(ends, row(r_end, MT, E), tile_no.unsqueeze(2).broadcast_to([P, MT, E]), ALU.is_le))
            op(V.tensor_reduce(r_te, ends, AX_X, ALU.add))
            op(V.tensor_scalar(r_te, r_te, float(E - 1), None, ALU.min))
            op(V.tensor_copy(tile_exp[:, :], r_te))
            even = tile_no.rearrange("p (i s) -> p i s", s=2)[:, :, 0]
            op(V.tensor_scalar(r_te[:, 0:MT // 2], even, r_end[:, E - 1:E], None, ALU.is_lt))
            op(V.tensor_reduce(r_a[:, 0:1], r_te[:, 0:MT // 2], AX_X, ALU.add))
            op(V.tensor_copy(n_pairs[:, :], r_a[:, 0:1]))
            dve.sem_inc(S["tiles_ready"], 1)
            op(V.tensor_tensor(r_t1, r_end, r_nt, ALU.subtract))
            op(V.tensor_scalar(r_t1, r_t1, float(P), None, ALU.mult))
            op(V.tensor_tensor(r_sel, r_base[:, 0:NT, :], row(r_t1, NT, E), ALU.add))
            op(V.tensor_tensor(r_sel, r_sel, bank[:, 0, 0:NT * E].rearrange("p (t e) -> p t e", e=E), ALU.add))
            for j, hot in enumerate((r_h0, r_h1)):
                op(V.tensor_tensor(r_off, r_sel, hot, ALU.mult))
                op(V.tensor_reduce(r_slot[:, j * NT:(j + 1) * NT], r_off, AX_X, ALU.add))
            op(V.tensor_copy(slot_i[:, :, :].rearrange("p j t -> p (j t)"), r_slot))
            op(V.tensor_scalar(tile_of[:, :], slot_i[:, :, :].rearrange("p j t -> p (j t)"), P.bit_length() - 1, None,
                               ALU.arith_shift_right))
            op(V.tensor_copy(r_tile, tile_of[:, :]))
            op(V.scalar_tensor_tensor(r_row, r_tile, -float(P), r_slot, ALU.mult, ALU.add))
            op(V.tensor_tensor(at_tile, row(tile_no, 2 * NT, MT), r_tile.unsqueeze(2).broadcast_to([P, 2 * NT, MT]),
                               ALU.is_equal))
            for j in range(2):
                for w in range(2):
                    c.put(V.tensor_tensor(tile_id[:, j * NT:(j + 1) * NT, w, :], at_tile[:, j * NT:(j + 1) * NT, :],
                                          col(r_part[:, w * NT:(w + 1) * NT], MT), ALU.mult))
            op(V.tensor_tensor(at_row, row(row_no, 2 * NT, P), r_row.unsqueeze(2).broadcast_to([P, 2 * NT, P]),
                               ALU.is_equal))
            dve.sem_inc(S["r_ready"], 1)
            dve.wait_ge(S["r_m"], 3)
            op(V.tensor_copy(r_id, bank[:, 2, 0:2 * MT]))
            op(V.scalar_tensor_tensor(r_tok, r_id[:, 0:MT], float(P), r_id[:, MT:], ALU.mult, ALU.add))
            op(V.tensor_copy(slot_tok[:, 0:MT], r_tok))
            dve.sem_inc(S["tok_ready"], 1)
            for j, hot in enumerate((r_h0, r_h1)):
                op(V.tensor_tensor(r_off, r_p, hot, ALU.mult))
                op(V.tensor_reduce(wgt[:, j, :], r_off, AX_X, ALU.add))
            op(V.tensor_tensor(r_a, wgt[:, 0, :], wgt[:, 1, :], ALU.add))
            op(V.reciprocal(r_b, r_a))
            for j in range(2):
                op(V.tensor_tensor(wgt[:, j, :], wgt[:, j, :], r_b, ALU.mult))
            dve.wait_ge(S["tiles_ready"], 1)
            pairs_used = dve.value_load(n_pairs[0:1, 0:1], min_val=1, max_val=MT // 2)

            dve.sem_inc(S["act_done"], 2)
            dve.sem_inc(S["aT_sb"], 1)
            dve.sem_inc(S["y_hi"], 1)
            dve.sem_inc(S["xgT_hi"], 1)
            c.reset()

            def turned_hi(t, s):
                dve.wait_ge(S["xg_ps"], t + 3)
                dve.wait_ge(S["gu_mm"], t + 1)
                V.tensor_copy(xgT[:, s, 4:8, :], bank[:, 5, :].rearrange("p (k n) -> p k n", k=4))\
                    .then_inc(S["xgT_hi"], 1)

            turned_hi(0, 0)
            with dve.Fori(0, MT // 2) as i, dve.If(i < pairs_used):
                def swish(s):
                    t = 2 * i + s
                    dve.wait_ge(S["g_sig"], t + 3)
                    c.put(V.tensor_tensor(act_t[:, s, :], act_t[:, s, :], bank[:, 2 * s, :], ALU.mult))
                    c.wait()
                    V.tensor_tensor(act_t[:, s, :], act_t[:, s, :], bank[:, 2 * s + 1, :], ALU.mult)\
                        .then_inc(S["act_done"], 1)

                def tail(s):
                    t = 2 * i + s
                    dve.wait_ge(S["aT_ps"], t + 3)
                    dve.wait_ge(S["y_mm"], 2 * t + 2)
                    V.tensor_copy(actT[:, s, :, :], bank[:, 4, :].rearrange("p (k n) -> p k n", k=KF))\
                        .then_inc(S["aT_sb"], 1)

                def out_hi(s):
                    t = 2 * i + s
                    dve.wait_ge(S["y_mm"], 2 * t + 6)
                    dve.wait_ge(y_st[s], 16 * i + 16)
                    V.tensor_copy(y_t[:, s, 512:], bank[:, 7, :]).then_inc(S["y_hi"], 1)

                turned_hi(2 * i + 1, 1)
                swish(0)
                tail(0)
                swish(1)
                tail(1)
                out_hi(0)
                turned_hi(2 * i + 2, 0)
                out_hi(1)
                c.reset()
            join(dve, 5)

            for t in range(NT):
                n, kind = (P, 0) if t < NTP else (NS, 1)
                dve.wait_ge(S["y_first"], t + 1)
                yt = ya[0:n, t, :]
                op(V.scalar_tensor_tensor(yt, yb[0:n, t, :], wgt[0:n, 1, t:t + 1], yt, ALU.mult, ALU.add))
                gate = V.tensor_tensor(yt, yt, G2[0:n, kind, :], ALU.mult)
                if t in POOL_ADDS:
                    gate.then_inc(S["y_gated"], 1)
                else:
                    op(gate)
                    V.tensor_tensor(x1[0:n, t, :], x1[0:n, t, :], yt, ALU.add).then_inc(S["y_sum"], 1)


_INS = ['x_prompt', 'x_sample', 'cache_k', 'cache_v', 'state_conv', 'page_table', 'c_prompt', 'c_sample', 'w_ada',
        'b_ada', 'norm_mix', 'norm_ffn', 'w_in', 'q_norm', 'k_norm', 'sb_bias', 'conv_w', 'conv_b', 'conv_ln_g',
        'conv_ln_b', 'w_out', 'w_router', 'b_router', 'w_gate', 'w_up', 'w_down']


def kernel(**inputs):
    import numpy as _np
    import concourse.bacc as _bacc
    from concourse import mybir as _mybir
    from concourse.bass_utils import run_bass_kernel_spmd as _run

    nc = _bacc.Bacc("TRN2", target_bir_lowering=False, num_devices=1)
    arrays, args = {}, []
    for name in _INS:
        a = _np.ascontiguousarray(inputs[name])
        arrays[f"in_{name}_dram"] = a
        args.append(nc.dram_tensor(f"in_{name}_dram", a.shape, _mybir.dt.from_np(a.dtype), kind="ExternalInput").ap())
    depth, _, _, heads, hd = inputs['cache_k'].shape
    bp, seq, _ = inputs['x_prompt'].shape
    bsm, dseq, _ = inputs['x_sample'].shape
    _, cwid, cch = inputs['conv_w'].shape
    outs = [inputs['x_prompt'].shape, inputs['x_sample'].shape, (depth, bp, seq, heads, hd), (depth, bp, seq, heads, hd),
            (depth, bp, cwid - 1, cch), (depth, bsm, dseq, heads, hd), (depth, bsm, dseq, heads, hd),
            (depth, bsm, cwid - 1, cch)]
    for i, shape in enumerate(outs):
        args.append(nc.dram_tensor(f"out_{i}_dram", shape, _mybir.dt.float32, kind="ExternalOutput").ap())
    decoder_step(nc, *args)
    r = _run(nc, [arrays], core_ids=[0])
    return tuple(r.results[0][f"out_{i}_dram"] for i in range(len(outs)))
```
